# Optimizing a Trainium2 kernel written in Bass

```python
import jax, jax.numpy as jnp
from jax import lax
import numpy as np
import math

D_MODEL = 1024
BATCH = 1
SEQ = 256
DEPTH = 2

CHUNK = 64
Q_BLOCK = 128
N_A_LAYERS = (DEPTH + 1) // 2
N_B_LAYERS = DEPTH - N_A_LAYERS
A_HEADS = 16
A_HEAD_DIM = D_MODEL // A_HEADS
B_HEADS = 16
NOPE_DIM = 64
ROPE_DIM = 32
V_DIM = 64
Q_RANK = 768
KV_RANK = 256
ROPE_THETA = 10000.0
N_EXPERTS = 16
N_GROUPS = 4
EXPERTS_PER_GROUP = N_EXPERTS // N_GROUPS
GROUP_SCORE_TOP = 2
TOP_K = 2
D_EXPERT = 512
EPS = 1e-6


def rmsnorm(x, g):
    xf = x.astype(jnp.float32)
    y = xf * lax.rsqrt(jnp.mean(xf * xf, axis=-1, keepdims=True) + EPS)
    return y.astype(x.dtype) * g

def modulate(h, shift, scale):
    return h * (1 + scale[:, None, :]) + shift[:, None, :]

def rope_tables(positions, dtype):
    half = ROPE_DIM // 2
    inv_freq = ROPE_THETA ** (-jnp.arange(half, dtype=jnp.float32) / half)
    ang = positions.astype(jnp.float32)[..., None] * inv_freq
    return jnp.cos(ang).astype(dtype), jnp.sin(ang).astype(dtype)

def apply_rope(x, cos, sin):
    x1, x2 = jnp.split(x, 2, axis=-1)
    return jnp.concatenate([x1 * cos - x2 * sin, x2 * cos + x1 * sin], axis=-1)

def block_sweep(attend, seq):
    return jnp.concatenate([attend(i * Q_BLOCK, (i + 1) * Q_BLOCK) for i in range(seq // Q_BLOCK)], axis=1)

def forgetting_attention(h, w_in, b_f, w_o):
    B, S, D = h.shape
    proj = h @ w_in
    q, k, v, f_logit = jnp.split(proj, [D, 2 * D, 3 * D], axis=-1)
    q = q.reshape(B, S, A_HEADS, A_HEAD_DIM)
    k = k.reshape(B, S, A_HEADS, A_HEAD_DIM)
    v = v.reshape(B, S, A_HEADS, A_HEAD_DIM)
    log_f = jax.nn.log_sigmoid((f_logit + b_f).astype(jnp.float32))
    cum = jnp.cumsum(log_f, axis=1).transpose(0, 2, 1)
    scale = A_HEAD_DIM ** -0.5
    pos = jnp.arange(S)

    def attend(t0, t1):
        s = jnp.einsum('bqhd,bkhd->bhqk', q[:, t0:t1], k[:, :t1], preferred_element_type=jnp.float32) * scale
        s = s + cum[:, :, t0:t1, None] - cum[:, :, None, :t1]
        allowed = pos[t0:t1, None] >= pos[None, :t1]
        p = jax.nn.softmax(jnp.where(allowed, s, -jnp.inf), axis=-1)
        return jnp.einsum('bhqk,bkhd->bqhd', p.astype(v.dtype), v[:, :t1])

    o = block_sweep(attend, S).reshape(B, S, D)
    return o @ w_o

def mla_shared_kv(x, c_act, norm_g, w_mod, b_mod, w_down, latent_g, w_up, cos, sin):
    B, S, _ = x.shape
    shift, scale = jnp.split(c_act @ w_mod + b_mod, 2, axis=-1)
    h = modulate(rmsnorm(x, norm_g), shift, scale)
    c_kv, k_rope = jnp.split(h @ w_down, [KV_RANK], axis=-1)
    c_kv = rmsnorm(c_kv, latent_g)
    kv = (c_kv @ w_up).reshape(B, S, B_HEADS, NOPE_DIM + V_DIM)
    k_nope, v = jnp.split(kv, [NOPE_DIM], axis=-1)
    k_rope = apply_rope(k_rope, cos, sin)
    return k_nope, k_rope, v

def latent_attention(h, k_nope, k_rope, v, w_dq, q_g, w_uq, w_o, cos, sin):
    B, S, _ = h.shape
    cq = rmsnorm(h @ w_dq, q_g)
    q = (cq @ w_uq).reshape(B, S, B_HEADS, NOPE_DIM + ROPE_DIM)
    q_nope, q_rope = jnp.split(q, [NOPE_DIM], axis=-1)
    q_rope = apply_rope(q_rope, cos[:, :, None, :], sin[:, :, None, :])
    scale = (NOPE_DIM + ROPE_DIM) ** -0.5
    chunk_id = jnp.arange(S) // CHUNK

    def attend(t0, t1):
        s = jnp.einsum('bqhd,bkhd->bhqk', q_nope[:, t0:t1], k_nope[:, :t1], preferred_element_type=jnp.float32)
        s = s + jnp.einsum('bqhr,bkr->bhqk', q_rope[:, t0:t1], k_rope[:, :t1], preferred_element_type=jnp.float32)
        allowed = chunk_id[t0:t1, None] >= chunk_id[None, :t1]
        p = jax.nn.softmax(jnp.where(allowed, s * scale, -jnp.inf), axis=-1)
        return jnp.einsum('bhqk,bkhd->bqhd', p.astype(v.dtype), v[:, :t1])

    o = block_sweep(attend, S).reshape(B, S, B_HEADS * V_DIM)
    return o @ w_o

def grouped_moe(h, router_w, router_bias, w_gate, w_up, w_down):
    B, S, D = h.shape
    hf = h.reshape(-1, D)
    n = hf.shape[0]
    scores = jax.nn.sigmoid(jnp.matmul(hf, router_w, preferred_element_type=jnp.float32))
    sel = (scores + router_bias.astype(jnp.float32)).reshape(n, N_GROUPS, EXPERTS_PER_GROUP)
    group_score = lax.top_k(sel, GROUP_SCORE_TOP)[0].sum(-1)
    g = jnp.argmax(group_score, axis=-1)
    g_idx = jnp.broadcast_to(g[:, None, None], (n, 1, EXPERTS_PER_GROUP))
    in_group = jnp.take_along_axis(sel, g_idx, axis=1)[:, 0]
    _, local = lax.top_k(in_group, TOP_K)
    idx = g[:, None] * EXPERTS_PER_GROUP + local
    w = jnp.take_along_axis(scores, idx, axis=1)
    w = w / jnp.sum(w, axis=-1, keepdims=True)
    combine = jnp.sum(jax.nn.one_hot(idx, N_EXPERTS, dtype=jnp.float32) * w[..., None], axis=1).astype(h.dtype)
    y = jnp.zeros_like(hf)
    for e in range(N_EXPERTS):
        a = jax.nn.silu(hf @ w_gate[e]) * (hf @ w_up[e])
        y = y + combine[:, e:e + 1] * (a @ w_down[e])
    return y.reshape(B, S, D)

def first_inputs(seed: int = 0) -> dict:
    key = jax.random.key(seed)
    ks = iter(jax.random.split(key, 40))
    f32 = jnp.float32
    D = D_MODEL

    def w(shape, fan_in, gain=1.0):
        return gain * fan_in ** -0.5 * jax.random.normal(next(ks), shape, f32)

    def gain(shape):
        return 1.0 + 0.05 * jax.random.normal(next(ks), shape, f32)

    def small(shape, s):
        return s * jax.random.normal(next(ks), shape, f32)

    x = jax.random.normal(next(ks), (BATCH, SEQ, D), f32)
    c = jax.random.normal(next(ks), (BATCH, D), f32)
    offset = jax.random.randint(next(ks), (BATCH, 1), 0, 4096, dtype=jnp.int32)
    positions = (jnp.arange(SEQ, dtype=jnp.int32)[None, :] + offset).astype(jnp.int32)
    return {
        "x": x,
        "c": c,
        "positions": positions,
        "a_norm_g": gain((N_A_LAYERS, D)),
        "a_w_in": w((N_A_LAYERS, D, 3 * D + A_HEADS), D),
        "a_b_f": jax.random.uniform(next(ks), (N_A_LAYERS, A_HEADS), f32, 1.0, 5.0),
        "a_w_o": w((N_A_LAYERS, D, D), D),
        "kv_norm_g": gain((D,)),
        "kv_w_mod": w((D, 2 * D), D, 0.5),
        "kv_b_mod": small((2 * D,), 0.02),
        "kv_w_down": w((D, KV_RANK + ROPE_DIM), D),
        "kv_latent_g": gain((KV_RANK,)),
        "kv_w_up": w((KV_RANK, B_HEADS * (NOPE_DIM + V_DIM)), KV_RANK),
        "b_norm_g": gain((N_B_LAYERS, D)),
        "b_w_dq": w((N_B_LAYERS, D, Q_RANK), D),
        "b_q_norm_g": gain((N_B_LAYERS, Q_RANK)),
        "b_w_uq": w((N_B_LAYERS, Q_RANK, B_HEADS * (NOPE_DIM + ROPE_DIM)), Q_RANK),
        "b_w_o": w((N_B_LAYERS, B_HEADS * V_DIM, D), B_HEADS * V_DIM),
        "w_mod": w((DEPTH, D, 6 * D), D, 0.5),
        "b_mod": small((DEPTH, 6 * D), 0.02),
        "ffn_norm_g": gain((DEPTH, D)),
        "router_w": w((D, N_EXPERTS), D),
        "router_bias": small((N_EXPERTS,), 0.01),
        "exp_w_gate": w((DEPTH, N_EXPERTS, D, D_EXPERT), D),
        "exp_w_up": w((DEPTH, N_EXPERTS, D, D_EXPERT), D),
        "exp_w_down": w((DEPTH, N_EXPERTS, D_EXPERT, D), D_EXPERT),
        "final_norm_g": gain((D,)),
    }

def first_block(x, c, positions, a_norm_g, a_w_in, a_b_f, a_w_o, kv_norm_g, kv_w_mod, kv_b_mod,
              kv_w_down, kv_latent_g, kv_w_up, b_norm_g, b_w_dq, b_q_norm_g, b_w_uq, b_w_o,
              w_mod, b_mod, ffn_norm_g, router_w, router_bias, exp_w_gate, exp_w_up, exp_w_down,
              final_norm_g):
    c_act = jax.nn.silu(c)
    cos, sin = rope_tables(positions, x.dtype)
    shared_kv = None
    for layer in range(DEPTH):
        sh1, sc1, g1, sh2, sc2, g2 = jnp.split(c_act @ w_mod[layer] + b_mod[layer], 6, axis=-1)
        if layer < N_A_LAYERS:
            h = modulate(rmsnorm(x, a_norm_g[layer]), sh1, sc1)
            mix = forgetting_attention(h, a_w_in[layer], a_b_f[layer], a_w_o[layer])
        else:
            j = layer - N_A_LAYERS
            h = modulate(rmsnorm(x, b_norm_g[j]), sh1, sc1)
            k_nope, k_rope, v = shared_kv
            mix = latent_attention(h, k_nope, k_rope, v, b_w_dq[j], b_q_norm_g[j], b_w_uq[j], b_w_o[j], cos, sin)
        x = x + g1[:, None, :] * mix
        h = modulate(rmsnorm(x, ffn_norm_g[layer]), sh2, sc2)
        x = x + g2[:, None, :] * grouped_moe(h, router_w, router_bias, exp_w_gate[layer], exp_w_up[layer], exp_w_down[layer])
        if layer == N_A_LAYERS - 1:
            shared_kv = mla_shared_kv(x, c_act, kv_norm_g, kv_w_mod, kv_b_mod, kv_w_down, kv_latent_g, kv_w_up, cos, sin)
    return rmsnorm(x, final_norm_g)


DEPTH_2 = 1

SSM_WIDTH = D_MODEL // 2
SSM_GROUP = 16
SSM_GROUPS = SSM_WIDTH // SSM_GROUP
SSM_STATE = 64
DT_MIN = 1e-3
DT_MAX = 1e-1
ATTN_HEADS = 8
ATTN_KV_HEADS = 2
HEAD_DIM = 64
ATTN_WIDTH = ATTN_HEADS * HEAD_DIM
IDX_HEADS = 8
IDX_DIM = 32
TOPK_MAX = 256
NEG_BIG = -1e30
PEER_HEADS = 8
PEER_KEYS = 128
PEER_EXPERTS = PEER_KEYS * PEER_KEYS
PEER_KEY_DIM = 128
PEER_TOPK = 16
PEER_CHUNK = 128
NORM_EPS = 1e-6

IN_SPLITS = (SSM_WIDTH, ATTN_WIDTH, ATTN_KV_HEADS * HEAD_DIM, ATTN_KV_HEADS * HEAD_DIM,
             IDX_HEADS * IDX_DIM, IDX_DIM, IDX_HEADS, D_MODEL, D_MODEL)
IN_WIDTH = sum(IN_SPLITS)


def rmsnorm_2(x, g):
    xf = x.astype(jnp.float32)
    y = xf * lax.rsqrt(jnp.mean(xf * xf, axis=-1, keepdims=True) + NORM_EPS)
    return (y * g.astype(jnp.float32)).astype(x.dtype)

def rope_tables_2(seq, dim):
    pos = jnp.arange(seq, dtype=jnp.float32)
    inv = ROPE_THETA ** (-jnp.arange(0, dim, 2, dtype=jnp.float32) / dim)
    ang = pos[:, None] * inv[None, :]
    return jnp.cos(ang), jnp.sin(ang)

def apply_rope_2(x, cos, sin):
    half = x.shape[-1] // 2
    shape = (cos.shape[0],) + (1,) * (x.ndim - 3) + (half,)
    c = cos.reshape(shape)
    s = sin.reshape(shape)
    xf = x.astype(jnp.float32)
    x1, x2 = xf[..., :half], xf[..., half:]
    return jnp.concatenate([x1 * c - x2 * s, x2 * c + x1 * s], axis=-1).astype(x.dtype)

def s5_branch(u, a_re, a_im, log_dt, b_re, b_im, c_re, c_im, d_skip, w_glu):
    bsz, seq, _ = u.shape
    f32 = jnp.float32
    uf = u.astype(f32).reshape(bsz, seq, SSM_GROUPS, SSM_GROUP)
    lam = lax.complex(a_re.astype(f32), a_im.astype(f32))
    dt = jnp.exp(log_dt.astype(f32))[:, None]
    a_bar = jnp.exp(lam * dt)
    b = lax.complex(b_re.astype(f32), b_im.astype(f32))
    b_bar = ((a_bar - 1.0) / lam)[..., None] * b
    bu = jnp.einsum('gpc,bsgc->bsgp', b_bar, uf)
    a_seq = jnp.broadcast_to(a_bar, bu.shape)

    def combine(left, right):
        a1, s1 = left
        a2, s2 = right
        return a2 * a1, a2 * s1 + s2

    _, states = lax.associative_scan(combine, (a_seq, bu), axis=1)
    c = lax.complex(c_re.astype(f32), c_im.astype(f32))
    y = jnp.real(jnp.einsum('gcp,bsgp->bsgc', c, states))
    y = y + d_skip.astype(f32).reshape(SSM_GROUPS, SSM_GROUP) * uf
    y = jax.nn.gelu(y.reshape(bsz, seq, SSM_WIDTH))
    y = y * jax.nn.sigmoid(y @ w_glu.astype(f32))
    return y.astype(u.dtype)

def dsa_branch(q, k, v, qi, ki, wi):
    bsz, seq = q.shape[0], q.shape[1]
    topk = min(TOPK_MAX, seq // 4)
    nb = seq // Q_BLOCK
    grp = ATTN_HEADS // ATTN_KV_HEADS
    f32 = jnp.float32
    kf = ki.astype(f32)
    idx_scale = (IDX_HEADS ** -0.5) * (IDX_DIM ** -0.5)
    s_pos = jnp.arange(seq)

    def to_blocks(t):
        return t.reshape((bsz, nb, Q_BLOCK) + t.shape[2:]).swapaxes(0, 1)

    def one_block(args):
        qb, qib, wib, blk = args
        t_pos = blk * Q_BLOCK + jnp.arange(Q_BLOCK)
        rel = jax.nn.relu(jnp.einsum('bthd,bsd->bths', qib.astype(f32), kf))
        score = jnp.einsum('bths,bth->bts', rel, wib.astype(f32)) * idx_scale
        causal = s_pos[None, :] <= t_pos[:, None]
        score = jnp.where(causal[None], score, NEG_BIG)
        _, sel = lax.top_k(score, topk)
        valid = sel <= t_pos[None, :, None]
        kg = jax.vmap(lambda kk, ii: kk[ii])(k, sel)
        vg = jax.vmap(lambda vv, ii: vv[ii])(v, sel)
        qg = qb.reshape(bsz, Q_BLOCK, ATTN_KV_HEADS, grp, HEAD_DIM).astype(f32)
        logits = jnp.einsum('btngd,btknd->btngk', qg, kg.astype(f32)) * (HEAD_DIM ** -0.5)
        logits = jnp.where(valid[:, :, None, None, :], logits, NEG_BIG)
        p = jax.nn.softmax(logits, axis=-1)
        o = jnp.einsum('btngk,btknd->btngd', p, vg.astype(f32))
        return o.reshape(bsz, Q_BLOCK, ATTN_WIDTH).astype(qb.dtype)

    out = lax.map(one_block, (to_blocks(q), to_blocks(qi), to_blocks(wi), jnp.arange(nb)))
    return out.swapaxes(0, 1).reshape(bsz, seq, ATTN_WIDTH)

def peer_ffn(x, w_q, sub_k1, sub_k2, u_tab, v_tab):
    bsz, seq, d = x.shape
    f32 = jnp.float32
    q = (x @ w_q).astype(f32).reshape(bsz, seq, PEER_HEADS, 2, PEER_KEY_DIM)
    s1 = jnp.einsum('bshd,hnd->bshn', q[..., 0, :], sub_k1.astype(f32))
    s2 = jnp.einsum('bshd,hnd->bshn', q[..., 1, :], sub_k2.astype(f32))
    v1, i1 = lax.top_k(s1, PEER_TOPK)
    v2, i2 = lax.top_k(s2, PEER_TOPK)
    cand_s = (v1[..., :, None] + v2[..., None, :]).reshape(bsz, seq, PEER_HEADS, PEER_TOPK * PEER_TOPK)
    cand_i = (i1[..., :, None] * PEER_KEYS + i2[..., None, :]).reshape(bsz, seq, PEER_HEADS, PEER_TOPK * PEER_TOPK)
    top_s, pos = lax.top_k(cand_s, PEER_TOPK)
    experts = jnp.take_along_axis(cand_i, pos, axis=-1)
    gates = jax.nn.softmax(top_s, axis=-1)
    n_tok = bsz * seq
    n_chunks = n_tok // PEER_CHUNK
    n_sel = PEER_HEADS * PEER_TOPK
    xc_all = x.reshape(n_chunks, PEER_CHUNK, d)
    ec_all = experts.reshape(n_chunks, PEER_CHUNK, n_sel)
    gc_all = gates.reshape(n_chunks, PEER_CHUNK, n_sel)

    def chunk(args):
        xc, ec, gc = args
        u = u_tab[ec].astype(f32)
        act = jax.nn.gelu(jnp.einsum('ced,cd->ce', u, xc.astype(f32))) * gc
        return jnp.einsum('ce,ced->cd', act, v_tab[ec].astype(f32)).astype(x.dtype)

    out = lax.map(chunk, (xc_all, ec_all, gc_all))
    return out.reshape(bsz, seq, d)

def second_inputs(seed: int = 0) -> dict:
    key = jax.random.key(seed)
    ks = jax.random.split(key, 24)
    f32 = jnp.float32
    L, D, G, P, N = DEPTH_2, D_MODEL, SSM_GROUPS, SSM_STATE, SSM_GROUP
    nrm = lambda k, shape, s: jax.random.normal(k, shape, f32) * s
    x = jax.random.normal(ks[0], (BATCH, SEQ, D), f32)
    norm1_g = 1.0 + nrm(ks[1], (L, D), 0.02)
    w_in = nrm(ks[2], (L, D, IN_WIDTH), D ** -0.5)
    a_re = -0.5 * (1.0 + nrm(ks[3], (L, G, P), 0.01))
    a_im = jnp.broadcast_to(math.pi * jnp.arange(P, dtype=f32), (L, G, P)) + nrm(ks[4], (L, G, P), 0.01)
    log_dt = jax.random.uniform(ks[5], (L, G), f32, math.log(DT_MIN), math.log(DT_MAX))
    b_re = nrm(ks[6], (L, G, P, N), (2.0 * N) ** -0.5)
    b_im = nrm(ks[7], (L, G, P, N), (2.0 * N) ** -0.5)
    c_re = nrm(ks[8], (L, G, N, P), P ** -0.5)
    c_im = nrm(ks[9], (L, G, N, P), P ** -0.5)
    d_skip = nrm(ks[10], (L, SSM_WIDTH), 1.0)
    w_glu = nrm(ks[11], (L, SSM_WIDTH, SSM_WIDTH), SSM_WIDTH ** -0.5)
    w_ssm_up = nrm(ks[12], (L, SSM_WIDTH, D), SSM_WIDTH ** -0.5)
    w_attn_up = nrm(ks[13], (L, ATTN_WIDTH, D), ATTN_WIDTH ** -0.5)
    w_out = nrm(ks[14], (L, D, D), D ** -0.5)
    norm2_g = 1.0 + nrm(ks[15], (L, D), 0.02)
    peer_wq = nrm(ks[16], (L, D, PEER_HEADS * 2 * PEER_KEY_DIM), D ** -0.5)
    peer_k1 = nrm(ks[17], (L, PEER_HEADS, PEER_KEYS, PEER_KEY_DIM), PEER_KEY_DIM ** -0.5)
    peer_k2 = nrm(ks[18], (L, PEER_HEADS, PEER_KEYS, PEER_KEY_DIM), PEER_KEY_DIM ** -0.5)
    peer_u = nrm(ks[19], (L, PEER_EXPERTS, D), D ** -0.5)
    peer_v = nrm(ks[20], (L, PEER_EXPERTS, D), PEER_HEADS ** -0.5)
    norm_f_g = 1.0 + nrm(ks[21], (D,), 0.02)
    return {"x": x, "norm1_g": norm1_g, "w_in": w_in, "a_re": a_re, "a_im": a_im,
            "log_dt": log_dt, "b_re": b_re, "b_im": b_im, "c_re": c_re, "c_im": c_im,
            "d_skip": d_skip, "w_glu": w_glu, "w_ssm_up": w_ssm_up, "w_attn_up": w_attn_up,
            "w_out": w_out, "norm2_g": norm2_g, "peer_wq": peer_wq, "peer_k1": peer_k1,
            "peer_k2": peer_k2, "peer_u": peer_u, "peer_v": peer_v, "norm_f_g": norm_f_g}

def second_block(x, norm1_g, w_in, a_re, a_im, log_dt, b_re, b_im, c_re, c_im, d_skip, w_glu,
              w_ssm_up, w_attn_up, w_out, norm2_g, peer_wq, peer_k1, peer_k2, peer_u, peer_v,
              norm_f_g):
    bsz, seq, _ = x.shape
    cos_a, sin_a = rope_tables_2(seq, HEAD_DIM)
    cos_i, sin_i = rope_tables_2(seq, IDX_DIM)
    offsets = np.cumsum(IN_SPLITS)[:-1].tolist()
    h = x
    for layer in range(DEPTH_2):
        xn = rmsnorm_2(h, norm1_g[layer])
        proj = xn @ w_in[layer]
        u, q, k, v, qi, ki, wi, g_ssm, g_attn = jnp.split(proj, offsets, axis=-1)
        y_ssm = s5_branch(u, a_re[layer], a_im[layer], log_dt[layer], b_re[layer], b_im[layer],
                          c_re[layer], c_im[layer], d_skip[layer], w_glu[layer])
        q = apply_rope_2(q.reshape(bsz, seq, ATTN_HEADS, HEAD_DIM), cos_a, sin_a)
        k = apply_rope_2(k.reshape(bsz, seq, ATTN_KV_HEADS, HEAD_DIM), cos_a, sin_a)
        v = v.reshape(bsz, seq, ATTN_KV_HEADS, HEAD_DIM)
        qi = apply_rope_2(qi.reshape(bsz, seq, IDX_HEADS, IDX_DIM), cos_i, sin_i)
        ki = apply_rope_2(ki, cos_i, sin_i)
        y_attn = dsa_branch(q, k, v, qi, ki, wi)
        merged = (jax.nn.sigmoid(g_ssm) * (y_ssm @ w_ssm_up[layer])
                  + jax.nn.sigmoid(g_attn) * (y_attn @ w_attn_up[layer]))
        h = h + merged @ w_out[layer]
        hn = rmsnorm_2(h, norm2_g[layer])
        h = h + peer_ffn(hn, peer_wq[layer], peer_k1[layer], peer_k2[layer], peer_u[layer], peer_v[layer])
    return rmsnorm_2(h, norm_f_g)


def setup_inputs(seed=0):
    out = dict(first_inputs(seed))
    for name, value in second_inputs(seed + 1).items():
        if name != "x":
            out[name + "_2"] = value
    return out


def reference(
    x, c, positions, a_norm_g, a_w_in, a_b_f, a_w_o, kv_norm_g, kv_w_mod, kv_b_mod, kv_w_down,
    kv_latent_g, kv_w_up, b_norm_g, b_w_dq, b_q_norm_g, b_w_uq, b_w_o, w_mod, b_mod, ffn_norm_g,
    router_w, router_bias, exp_w_gate, exp_w_up, exp_w_down, final_norm_g, norm1_g_2, w_in_2,
    a_re_2, a_im_2, log_dt_2, b_re_2, b_im_2, c_re_2, c_im_2, d_skip_2, w_glu_2, w_ssm_up_2,
    w_attn_up_2, w_out_2, norm2_g_2, peer_wq_2, peer_k1_2, peer_k2_2, peer_u_2, peer_v_2,
    norm_f_g_2,
):
    x = first_block(
        x, c, positions, a_norm_g, a_w_in, a_b_f, a_w_o, kv_norm_g, kv_w_mod, kv_b_mod,
        kv_w_down, kv_latent_g, kv_w_up, b_norm_g, b_w_dq, b_q_norm_g, b_w_uq, b_w_o, w_mod,
        b_mod, ffn_norm_g, router_w, router_bias, exp_w_gate, exp_w_up, exp_w_down,
        final_norm_g,
    )
    return second_block(
        x, norm1_g_2, w_in_2, a_re_2, a_im_2, log_dt_2, b_re_2, b_im_2, c_re_2, c_im_2,
        d_skip_2, w_glu_2, w_ssm_up_2, w_attn_up_2, w_out_2, norm2_g_2, peer_wq_2, peer_k1_2,
        peer_k2_2, peer_u_2, peer_v_2, norm_f_g_2,
    )


_drawn_inputs = setup_inputs


def setup_inputs(seed=0):
    import zlib

    import numpy as np

    out = dict(_drawn_inputs(seed))
    spreads = {}
    factors = {'b_norm_g': 4.87,
     'b_q_norm_g': 4.982,
     'a_re_2': 200.0,
     'norm_f_g_2': 22.822,
     'a_im_2': 30.016,
     'log_dt_2': 31.6,
     'b_re_2': 34.04,
     'b_im_2': 34.744,
     'c_re_2': 35.632,
     'c_im_2': 33.36}
    for name, (base, spread) in spreads.items():
        noise = np.random.default_rng([zlib.crc32(name.encode()), seed]).standard_normal(out[name].shape)
        drawn = base * np.exp(spread * noise) if base else spread * noise
        out[name] = __import__('jax').numpy.asarray(drawn.astype(out[name].dtype))
    for name, factor in factors.items():
        out[name] = (out[name] * factor).astype(out[name].dtype)
    return out
```

```python
import math
from contextlib import ExitStack

import numpy as np

import concourse.bass as bass
from concourse import mybir

T, D = 256, 1024
P = 128
C = T // P
DB = D // P
HEADS, HD = 16, 64
NOPE, ROPE = 64, 32
QK = NOPE + ROPE
QR, KVR = 768, 256
NE, DE = 16, 512
EB = DE // P
NG, EPG = 4, 4
SSM_W, SSM_G, SSM_P, SSM_N = 512, 32, 64, 16
ST = SSM_G * SSM_P // P
AH, KVH, IH, ID = 8, 2, 8, 32
TOPK = 64
PH, PK, PD, PT_ = 8, 128, 128, 16
SEL = PH * PT_
EPS = 1e-6
BIG = 3.0e38
NEG = -1.0e30
TWO_PI_A, TWO_PI_B = 6.28125, 0.0019350051879882812
TWO_PI_C = 2 * math.pi - TWO_PI_A - TWO_PI_B
ROUND = 12582912.0
PI = 3.1415925

K_ID, K_TRI, K_ONE = 0, 128, 256
K_CAUSAL = 384
K_CHUNK = K_CAUSAL + 384
K_COS64 = K_CHUNK + 384
K_SIN64 = K_COS64 + 64
K_COS32 = K_SIN64 + 64
K_SIN32 = K_COS32 + 32
K_INV = K_SIN32 + 32
K_IOTA = K_INV + 16
K_N = K_IOTA + 16


def shape_constants():
    k = np.zeros((P, K_N), np.float32)
    p = np.arange(P)
    k[:, K_ID:K_ID + P] = np.eye(P)
    k[:, K_TRI:K_TRI + P] = p[:, None] <= p[None, :]
    k[:, K_ONE:K_ONE + P] = 1
    for base, unit in ((K_CAUSAL, 1), (K_CHUNK, 64)):
        for c in range(C):
            at = base + P * c
            keys = np.arange(P * (c + 1))
            ok = (p[:, None] + P * c) // unit >= keys[None, :] // unit
            k[:, at:at + P * (c + 1)] = np.where(ok, np.float32(BIG), np.float32(NEG))
    for base_c, base_s, dim in ((K_COS64, K_SIN64, 64), (K_COS32, K_SIN32, 32)):
        inv = np.float32(10000.0) ** (-np.arange(0, dim, 2, dtype=np.float32) / np.float32(dim))
        for c in range(C):
            ang = (p + P * c).astype(np.float32)[:, None] * inv.astype(np.float32)[None, :]
            h = dim // 2
            k[:, base_c + h * c:base_c + h * (c + 1)] = np.cos(ang)
            k[:, base_s + h * c:base_s + h * (c + 1)] = np.sin(ang)
    k[:, K_INV:K_INV + 16] = np.float32(10000.0) ** (-np.arange(16, dtype=np.float32) / np.float32(16))
    k[:, K_IOTA:K_IOTA + 16] = np.arange(16)
    return k


def build(nc, A, out):
    fp32, i32, u32 = mybir.dt.float32, mybir.dt.int32, mybir.dt.uint32
    ALU = mybir.AluOpType
    ACT = mybir.ActivationFunctionType
    AX = mybir.AxisListType
    ctx = ExitStack()
    ctx.enter_context(nc.allow_non_contiguous_dma(reason="a few small parameters are laid out by their load"))
    sems, counts = {}, {}

    def S(name):
        if name not in sems:
            sems[name] = ctx.enter_context(nc.semaphore(name))
        return sems[name]

    def sb(name, shape, dt=fp32):
        return ctx.enter_context(nc.sbuf_tensor(name, shape, dt))

    RING, SLAB = 6, 4096
    ring = sb("ring", [P, RING * SLAB])
    consts = sb("consts", [P, K_N])
    X = sb("X", [P, C, D])
    Hm = sb("H", [P, C * D])
    HTm = sb("HT", [P, DB * T])
    MOD = sb("MOD", [P, 6 * D])
    GAIN = sb("GAIN", [P, D])
    AR = sb("AR", [P, 13312])
    cT = sb("cT", [P, DB])
    rope_cs = sb("rope_cs", [P, 2, C, 16])
    pos_i = sb("pos_i", [P, C], i32)
    rw = sb("rw", [P, DB, NE])
    rb = sb("rb", [P, NE])
    bf = sb("bf", [P, HEADS])
    st = sb("st", [P, 16])
    PS = ctx.enter_context(nc.psum_tensor("PS", [P, 8, 512], fp32))

    ident = consts[:, K_ID:K_ID + P]
    tri = consts[:, K_TRI:K_TRI + P]
    ones = consts[:, K_ONE:K_ONE + P]

    H = Hm[:, :].rearrange("p (c d) -> p c d", c=C)
    HT = HTm[:, :].rearrange("p (b t) -> p b t", t=T)

    def ar(at, *shape):
        n = int(np.prod(shape))
        return view(AR, at, *shape)

    def view(t, at, *shape):
        n = int(np.prod(shape))
        v = t[:, at:at + n]
        if len(shape) == 1:
            return v
        names = "abcd"[:len(shape)]
        return v.rearrange("p (" + " ".join(names) + ") -> p " + " ".join(names),
                           **{x: s for x, s in zip(names[1:], shape[1:])})

    slabs, pieces, stages = [], [], {}

    def stream(name, w, kb, cols, kind="N"):
        stages[name] = []
        for c0, n in cols:
            r = len(slabs)
            ps = [(o, min(512, n - o)) for o in range(0, n, 512)]
            for o, m in ps:
                stages[name].append((len(pieces), r, o, m, kind))
                pieces.append(name)
            slabs.append(dict(src=w[:, c0:c0 + n].rearrange("(b p) n -> p b n", p=P), kb=kb, n=n,
                              release=("gemm_done", len(pieces))))

    def stream_experts(layer):
        base = len(slabs)
        stages[f"moe{layer}"] = base
        last = NE // 2 - 1
        for it in range(NE // 2):
            for k in range(6):
                name = f"gu_done{layer}" if k < 4 else f"down_done{layer}"
                count = 8 * it + 4 * (k // 2 % 2) + 4 if k < 4 else 8 * it + 4 * (k - 4) + 4 + 8
                slabs.append(dict(layer=layer, it=it, k=k, release=(name, count)))

    def cols(n, step=512, at=0):
        return [(at + o, min(step, n - o)) for o in range(0, n, step)]

    stream("mod0", A["w_mod"][0], DB, cols(6 * D), "M")
    stream("a_qk", A["a_w_in"][0], DB, cols(2 * D), "T")
    stream("a_v", A["a_w_in"][0], DB, cols(D, at=2 * D) + [(3 * D, HEADS)])
    stream("a_o", A["a_w_o"][0], DB, cols(D))
    stream_experts(0)
    stream("kvmod", A["kv_w_mod"], DB, cols(2 * D), "M")
    stream("mod1", A["w_mod"][1], DB, cols(6 * D), "M")
    stream("kv_down", A["kv_w_down"], DB, [(0, KVR + ROPE)])
    stream("kv_up", A["kv_w_up"], KVR // P, [(0, 2 * D)])
    stream("b_dq", A["b_w_dq"][0], DB, cols(QR))
    stream("b_uq", A["b_w_uq"][0], QR // P, cols(HEADS * QK))
    stream("b_o", A["b_w_o"][0], DB, cols(D))
    stream_experts(1)
    stream("c_u", A["w_in_2"][0], DB, [(0, 512)])
    stream("c_p", A["w_in_2"][0], DB, [(512, 512), (1024, 512), (1536, 40)])
    stream("c_g", A["w_in_2"][0], DB, cols(2 * D, at=1576))
    stream("glu", A["w_glu_2"][0], SSM_W // P, [(0, SSM_W)])
    stream("ssm_up", A["w_ssm_up_2"][0], SSM_W // P, [(0, D)])
    stream("attn_up", A["w_attn_up_2"][0], SSM_W // P, [(0, D)])
    stream("c_o", A["w_out_2"][0], DB, cols(D))
    stream("peer_q", A["peer_wq_2"][0], DB, cols(2 * D), "T")

    evac_by = {"mod0": "v", "mod1": "v", "kvmod": "v"}
    evac_at, n_by = [], {"v": 0, "a": 0}
    for g, name in enumerate(pieces):
        e = evac_by.get(name, "a")
        n_by[e] += 1
        evac_at.append(("evac_" + e, n_by[e]))

    def slab_view(r, kb, n):
        return ring[:, (r % RING) * SLAB:(r % RING) * SLAB + kb * n].rearrange("p (b n) -> p b n", n=n)

    def slab_loaded(eng, r):
        eng.wait_ge(S(f"slab{r % RING}"), 16 * (r // RING + 1))

    def link(eng, ins, name):
        counts[name] = counts.get(name, 0) + 1
        ins.then_inc(S(name), 1)
        eng.wait_ge(S(name), counts[name])

    ATT = {
        "A": dict(Q=ar(0, 8, T), K=ar(2048, 8, T), V=ar(4096, C, D), O=ar(6144, 8, T), SC=ar(8192, 2, 1024),
                  PT=ar(10240, 2, 1024), heads=16, scale=1.0, mask=K_CAUSAL),
        "B": dict(Q=ar(7168, 16, T), K=ar(3072, 16, T), V=ar(11264, C, D), O=HT, SC=ar(0, 2, 1024),
                  PT=view(Hm, 0, 2, 1024), heads=16, scale=float(QK) ** -0.5, mask=K_CHUNK),
        "C": dict(Q=ar(6224, 4, T), K=ar(7248, 2, T), V=ar(0, C, 1064), O=ar(8528, 4, T), SC=ar(9552, 2, 1024),
                  PT=view(HTm, 0, 2, 1024), heads=8, scale=0.125, mask=None),
    }
    F, Ft, Fn = ar(12288, C, HEADS), ar(12320, C, HEADS), ar(12352, C, HEADS)
    NCT = ar(12384, T)
    Y, AT, SG = ar(0, C, D), ar(2048, 2, EB, T), ar(4096, 4, T)
    RSC, RSEL, COMB = ar(5120, C, NE), ar(5152, C, NE), ar(5184, C, NE)
    RT = ar(5216, 512)
    RIDX = AR[:, 5728:5744].bitcast(u32).rearrange("p (c k) -> p c k", c=C)
    KM = ar(11264, 2 * D)
    KTOK = ar(0, C, HEADS, QK)
    CKV, CKVT = ar(7168, C, KVR + ROPE), ar(7744, 2, T)
    CQ, CQT = ar(0, C, QR), view(Hm, 0, QR // P, T)
    QTOK = ar(0, C, HEADS, QK)
    PROJ, U, UT = ar(0, C, 1064), ar(2128, C, SSM_W), ar(3152, 4, T)
    Y5, Y5T = ar(4176, C, SSM_W), ar(5200, 4, T)
    GATES = view(MOD, 0, C, 2 * D)
    BN = [ar(6224, ST, 32), ar(6736, ST, 32)]
    CN = [ar(7248, 4, P), ar(7760, 4, P)]
    BT = [ar(8272, 4, P), ar(8784, 4, P)]
    CT = [ar(9296, 4, P), ar(9808, 4, P)]
    Er, Ei = ar(6224, 4, T), ar(7248, 4, T)
    T1, T2 = ar(10320, 4, T), ar(11344, 4, T)
    Zr, Zi = view(MOD, 4096, 4, T), view(MOD, 5120, 4, T)
    Sr, Si = view(Hm, 0, 4, T), view(Hm, 1024, 4, T)
    SP_ = [ar(12368 + 16 * i, ST) for i in range(24)]
    KD = ar(11600, C, 2, 2, HD)
    KI4 = ar(12112, C, 4, ID)
    QIT, KIT = ar(7760, 2, T), ar(8272, T)
    RELU = view(Hm, 0, IH, T)
    SCORE, SLEFT = ar(12368, T), ar(12624, T)
    T8, WI = ar(12880, 8), ar(12888, IH)
    MASKC = ar(11600, C, T)
    M1, M2 = ar(9552, C, D), view(Hm, 0, C, D)
    PQT, KT, PSC = ar(0, 16, T), ar(4096, 16, PK), ar(6144, 16, PK)
    CAND, PTMP = ar(8192, PH, PT_ * PT_), ar(10240, PH * PT_, PT_)
    KN = view(MOD, 0, 16, PD)
    V16, I16F = view(MOD, 2048, 16, PT_), view(MOD, 2304, 16, PT_)
    I16 = MOD[:, 2560:2816].bitcast(u32).rearrange("p (b k) -> p b k", b=16)
    TV, TP_ = view(MOD, 2816, PH, PT_), MOD[:, 2944:3072].bitcast(u32).rearrange("p (b k) -> p b k", b=PH)
    HI, LO = MOD[:, 3072:3200].bitcast(u32), MOD[:, 3200:3328].bitcast(u32)
    HIF, LOF = view(MOD, 3328, SEL), view(MOD, 3456, SEL)
    EHI, ELO = view(MOD, 3584, SEL), view(MOD, 3712, SEL)
    EXPERT = MOD[:, 3840:4096].bitcast(u32).rearrange("p (c k) -> p c k", c=C)
    GATE, DOT = view(MOD, 4096, C, SEL), view(MOD, 4352, C, SEL)
    PSUMS = view(MOD, 4608, PH)
    PICK = [MOD[:, 4624 + 8 * i:4632 + 8 * i].bitcast(u32) for i in range(2)]

    TPJ, tp_n = {}, [0]

    def tp_job(name, batches):
        TPJ[name] = (tp_n[0], batches)
        tp_n[0] += len(batches)

    def tp_end(name):
        return TPJ[name][0] + len(TPJ[name][1])

    def both_chunks(name, src, dst, nb, w=P):
        bs = []
        for f in range(0, nb, 2):
            m = min(2, nb - f)
            bs.append(([src[:, c, w * (f + i):w * (f + i + 1)] for i in range(m) for c in range(C)],
                       dst[0:w, f:f + m, :].rearrange("p a t -> p (a t)"), 1.0))
        tp_job(name, bs)

    flat = "p c h d -> p c (h d)"
    both_chunks("h_a", H, HT, DB)
    tp_job("cum", [([Fn[:, c, :] for c in range(C)], NCT[0:HEADS, :], 1.0)])
    both_chunks("h_ffn0", H, HT, DB)
    both_chunks("h_kv", H, HT, DB)
    both_chunks("ckv", CKV, CKVT, 2)
    both_chunks("kB", KTOK.rearrange(flat), ATT["B"]["K"], HEADS, QK)
    both_chunks("h_b", H, HT, DB)
    both_chunks("cq", CQ, CQT, QR // P)
    both_chunks("qB", QTOK.rearrange(flat), ATT["B"]["Q"], HEADS, QK)
    both_chunks("h_ffn1", H, HT, DB)
    both_chunks("h_n1", H, HT, DB)
    tp_job("ssm_w", [([BN[x][:, 4 * b:4 * b + 4, :].rearrange("p a d -> p (a d)") for b in range(4)],
                      BT[x].rearrange("p a d -> p (a d)"), 1.0) for x in range(2)] +
           [([CN[x][:, b, :] for b in range(4)], CT[x].rearrange("p a d -> p (a d)"), 1.0 - 2 * x)
            for x in range(2)])
    both_chunks("u", U, UT, 4)
    both_chunks("y5", Y5, Y5T, 4)
    both_chunks("y5g", Y5, Y5T, 4)
    both_chunks("qC", PROJ, ATT["C"]["Q"], 4)
    both_chunks("kC", KD.rearrange("p c a b d -> p c (a b d)"), ATT["C"]["K"], 2)
    both_chunks("qi", PROJ[:, :, 768:1024], QIT, 2)
    both_chunks("ki", KI4.rearrange(flat), KIT.rearrange("p (a t) -> p a t", a=1), 1)
    both_chunks("merged", M1, HT, DB)
    tp_job("peer_k", [([KN[:, 4 * b + i, :] for i in range(4)],
                       KT[:, 4 * b:4 * b + 4, :].rearrange("p a d -> p (a d)"), 1.0) for b in range(4)])
    both_chunks("h_n2", H, HT, DB)

    gain_list = [("a", A["a_norm_g"][0]), ("ffn0", A["ffn_norm_g"][0]), ("kv", A["kv_norm_g"]),
                 ("latent", A["kv_latent_g"]), ("b", A["b_norm_g"][0]), ("q", A["b_q_norm_g"][0]),
                 ("ffn1", A["ffn_norm_g"][1]), ("final", A["final_norm_g"]), ("n1", A["norm1_g_2"][0]),
                 ("dskip", A["d_skip_2"][0]), ("n2", A["norm2_g_2"][0]), ("nf", A["norm_f_g_2"])]
    gain_no = {n: i for i, (n, _) in enumerate(gain_list)}
    h_no = {n: i + 1 for i, n in enumerate(["a", "ffn0", "kv", "b", "ffn1", "n1", "n2"])}
    x_no = {n: i + 1 for i, n in enumerate(["a_o", "moe0", "b_o", "moe1", "final", "c_o", "peer"])}

    block = ctx.enter_context(nc.Block())

    def rows(w):
        return w.rearrange("(c p) d -> p c d", p=P)

    @block.sync
    def _(sp):
        sp.dma_start(consts[:, :], A["consts"]).then_inc(S("consts_in"), 16)
        sp.dma_start(cT[:, :], A["c"][0].rearrange("(b p) -> p b", p=P)).then_inc(S("c_in"), 16)
        sp.dma_start(X[:, :, :], rows(A["x"][0])).then_inc(S("x_in"), 16)

        def released(r):
            sp.wait_ge(S(slabs[r - RING]["release"][0]), slabs[r - RING]["release"][1])

        r = 0
        while r < len(slabs):
            s = slabs[r]
            if "layer" not in s:
                if r >= RING:
                    released(r)
                sp.dma_start(slab_view(r, s["kb"], s["n"]), s["src"]).then_inc(S(f"slab{r % RING}"), 16)
                r += 1
                continue
            layer = s["layer"]
            srcs = [A[n][layer] for n in ("exp_w_gate", "exp_w_up") * 2 + ("exp_w_down",) * 2]
            which = [0, 0, 1, 1, 0, 1]

            def load_expert(k, e):
                kb, n = (EB, D) if k >= 4 else (DB, DE)
                sp.dma_start(slab_view(r + k, kb, n), srcs[k][e].rearrange("(b p) n -> p b n", p=P)
                             ).then_inc(S(f"slab{(r + k) % RING}"), 16)

            for k in range(RING):
                released(r + k)
                load_expert(k, which[k])
            with sp.Fori(1, NE // 2) as it:
                for k in range(RING):
                    if k < 4:
                        sp.wait_ge(S(f"gu_done{layer}"), it * 8 + (4 * (k // 2) + 4 - 8))
                    else:
                        sp.wait_ge(S(f"down_done{layer}"), it * 8 + (4 * (k - 4) + 4))
                    load_expert(k, it * 2 + which[k])
            r += 6 * (NE // 2)
        sp.wait_ge(S("result"), 1)
        sp.dma_start(rows(out[0]), H).then_inc(S("out_written"), 16)
        sp.wait_ge(S("out_written"), 16)

    @block.gpsimd
    def _(pool):
        def bcast(dst, src, name):
            pool.dma_start(dst, src.partition_broadcast(P)).then_inc(S(name), 16)

        def load_gain(n):
            i = gain_no[n]
            if i:
                pool.wait_ge(S("gain_used"), i)
            src = gain_list[i][1]
            bcast(GAIN[:, 0:src.shape[0]], src, "gain_in")

        bcast(MOD[:, :], A["b_mod"][0], "modb_in")
        load_gain("a")
        bcast(bf[:, :], A["a_b_f"][0], "small_in")
        bcast(rb[:, :], A["router_bias"], "small_in")
        pool.dma_start(rw[:, :, :], A["router_w"].rearrange("(b p) n -> p b n", p=P)).then_inc(S("small_in"), 16)
        pool.dma_start(pos_i[:, :], A["positions"][0].rearrange("(c p) -> p c", p=P)).then_inc(S("small_in"), 16)
        load_gain("ffn0")
        load_gain("kv")
        pool.wait_ge(S("x_ready"), x_no["moe0"])
        bcast(KM, A["kv_b_mod"], "kvb_in")
        bcast(MOD[:, :], A["b_mod"][1], "modb_in")
        load_gain("latent")
        load_gain("b")
        load_gain("q")
        load_gain("ffn1")
        load_gain("final")
        load_gain("n1")
        pool.wait_ge(S("x_ready"), x_no["b_o"])
        for x in range(2):
            pool.memset(BN[x], 0.0).then_inc(S("ssm_zero"), 1)
            pool.memset(CN[x], 0.0).then_inc(S("ssm_zero"), 1)
        pool.wait_ge(S("ssm_zero"), 4)
        for x, (b_, c_) in enumerate((("b_re_2", "c_re_2"), ("b_im_2", "c_im_2"))):
            for g in range(2):
                pool.dma_start(BN[x][64 * g:64 * g + 64, :, 16 * g:16 * g + 16],
                               A[b_][0].rearrange("(t g) p n -> g p t n", g=2)[g]).then_inc(S("ssm_in"), 16)
            csrc = A[c_][0].rearrange("(b i g) n p -> i g n b p", b=4, i=4)
            for i in range(4):
                for g in range(2):
                    q = 32 * i + 16 * g
                    pool.dma_start(CN[x][q:q + 16, :, 64 * g:64 * g + 64], csrc[i, g]).then_inc(S("ssm_in"), 16)
        for g in range(2):
            q = slice(64 * g, 64 * g + 64)
            pool.dma_start(SP_[0][q, :], A["a_re_2"][0].rearrange("(t g) p -> g p t", g=2)[g]).then_inc(S("ssm_in"), 16)
            pool.dma_start(SP_[1][q, :], A["a_im_2"][0].rearrange("(t g) p -> g p t", g=2)[g]).then_inc(S("ssm_in"), 16)
            pool.dma_start(SP_[2][q, :], A["log_dt_2"][0].rearrange("(t g) -> g t", g=2)[g].partition_broadcast(64)
                           ).then_inc(S("ssm_in"), 16)
        load_gain("dskip")
        load_gain("n2")
        pool.wait_ge(S("x_ready"), x_no["c_o"])
        for half, k_ in enumerate(("peer_k1_2", "peer_k2_2")):
            pool.dma_start(KN[:, half::2, :], A[k_][0].rearrange("h n d -> n h d")).then_inc(S("peerk_in"), 16)
        load_gain("nf")
        pool.wait_ge(S("gemm_done"), len(pieces))
        for ph, (tab, c) in enumerate(((("peer_u_2", 0)), ("peer_u_2", 1), ("peer_v_2", 0), ("peer_v_2", 1))):
            pool.wait_ge(S("experts"), c + 1)
            if ph == 2:
                for half in range(2):
                    pool.wait_ge(S(f"rows_used{half}"), 2 * (SEL // 16) + 1)
            with pool.Fori(0, SEL // 16) as i:
                for half in range(2):
                    if ph < 2:
                        pool.wait_ge(S(f"rows_used{half}"), i + (8 * ph + 1))
                    else:
                        pool.wait_ge(S(f"x_acc{half}"), i * 8 + (64 * c + 1))
                    pool.tensor_copy(PICK[half], EXPERT[:, c, bass.ds(i * 16 + 8 * half, 8)]
                                     ).then_inc(S(f"picked{half}"), 1)
                    pool.wait_ge(S(f"picked{half}"), i + (8 * ph + 1))
                    pool.sem_inc(S("sets_asked"), 1)
                    for j in range(8):
                        at = (8 * half + j) * D
                        pool.indirect_dma_start(
                            out=ring[:, at:at + D], out_offset=None, in_=A[tab][0],
                            in_offset=bass.IndirectOffsetOnAxis(ap=PICK[half][:, j:j + 1], axis=0),
                        ).then_inc(S(f"rows_in{half}"), 16)

    @block.tensor
    def _(pe):
        def tp(name, *waits):
            for w, n in waits:
                pe.wait_ge(S(w), n)
            first, batches = TPJ[name]
            for b, (srcs, dst, _s) in enumerate(batches):
                n = first + b
                if n >= 4:
                    pe.wait_ge(S("tp_out"), n - 3)
                for i, src in enumerate(srcs):
                    w = src.shape[-1]
                    last = nc.tensor.transpose(PS[0:w, 4 + n % 4, P * i:P * i + P], src, ident)
                last.then_inc(S("tp_done"), 1)

        def gemm(name, lhs, *waits):
            for w, n in waits:
                pe.wait_ge(S(w), n)
            for g, r, off, n, kind in stages[name]:
                s = slabs[r]
                slab_loaded(pe, r)
                if g >= 2:
                    pe.wait_ge(S(evac_at[g - 2][0]), evac_at[g - 2][1])
                w = slab_view(r, s["kb"], s["n"])
                pair = 2 * (g % 2)
                if kind == "N":
                    for c in range(C):
                        for k in range(s["kb"]):
                            last = nc.tensor.matmul(PS[:, pair + c, 0:n], lhs[:, k, P * c:P * c + P],
                                                    w[:, k, off:off + n], start=k == 0, stop=k == s["kb"] - 1)
                elif kind == "T":
                    for f in range(n // P):
                        o = T * (f % 2)
                        for k in range(s["kb"]):
                            last = nc.tensor.matmul(PS[:, pair + f // 2, o:o + T], w[:, k, P * f:P * f + P],
                                                    lhs[:, k, :], start=k == 0, stop=k == s["kb"] - 1)
                else:
                    for k in range(s["kb"]):
                        last = nc.tensor.matmul(PS[:, pair, 0:n], cT[:, k:k + 1].to_broadcast((P, P)),
                                                w[:, k, off:off + n], start=k == 0, stop=k == s["kb"] - 1)
                last.then_inc(S("gemm_done"), 1)

        def ht(name):
            return ("tp_out", tp_end(name))

        def attention(a, first_waits, extra=None):
            z = ATT[a]
            for w, n in first_waits:
                pe.wait_ge(S(w), n)
            steps = [(g, c) for g in range(z["heads"] // 4) for c in range(C)]

            def scores(n):
                g, c = steps[n]
                if n >= 2:
                    pe.wait_ge(S(f"masked{a}"), n - 1)
                kl = P * (c + 1)
                for i in range(4):
                    h = 4 * g + i
                    o = PS[:, 2 * (n % 2) + i % 2, T * (i // 2):T * (i // 2) + kl]
                    if a == "B":
                        q, k = z["Q"][0:QK, h, P * c:P * c + P], z["K"][0:QK, h, 0:kl]
                    else:
                        b = slice(64 * (h % 2), 64 * (h % 2) + 64)
                        kb = h // 2 if a == "A" else h // 4
                        q, k = z["Q"][b, h // 2, P * c:P * c + P], z["K"][b, kb, 0:kl]
                    last = nc.tensor.matmul(o, q, k, start=True, stop=a != "A")
                    if a == "A":
                        last = nc.tensor.matmul(o, ident[0:HEADS, h:h + 1].to_broadcast((HEADS, P)),
                                                NCT[0:HEADS, 0:kl], start=False, stop=True)
                last.then_inc(S(f"scores{a}"), 1)

            def transposes(n):
                g, c = steps[n]
                pe.wait_ge(S(f"probs{a}"), n + 1)
                if n >= 1:
                    pe.wait_ge(S(f"pt{a}"), n)
                sc = z["SC"][:, n % 2, 0:4 * P * (c + 1)].rearrange("p (h k) -> p h k", h=4)
                for i in range(4):
                    for kc in range(c + 1):
                        m = i * (c + 1) + kc
                        last = nc.tensor.transpose(PS[:, 4 + m // 4, P * (m % 4):P * (m % 4) + P],
                                                   sc[:, i, P * kc:P * kc + P], ident)
                last.then_inc(S(f"ptp{a}"), 1)

            def values(n):
                g, c = steps[n]
                pe.wait_ge(S(f"pt{a}"), n + 1)
                if n >= 2:
                    pe.wait_ge(S(f"o{a}"), n - 1)
                for i in range(4):
                    h = 4 * g + i
                    for kc in range(c + 1):
                        m = (2 * (i % 2) + i // 2) * (c + 1) + kc
                        at = 640 + (h // 4) * 64 if a == "C" else h * 64
                        last = nc.tensor.matmul(
                            PS[64 * (i % 2):64 * (i % 2) + 64, 6 + n % 2, P * (i // 2):P * (i // 2) + P],
                            z["V"][:, kc, at:at + 64], z["PT"][:, n % 2, P * m:P * m + P],
                            start=kc == 0, stop=kc == c)
                last.then_inc(S(f"omm{a}"), 1)

            scores(0)
            for n in range(len(steps)):
                if n + 1 < len(steps):
                    scores(n + 1)
                transposes(n)
                if n >= 1:
                    values(n - 1)
            values(len(steps) - 1)

        def experts(layer):
            base = stages[f"moe{layer}"]
            pe.wait_ge(S("small_in"), 64)
            pe.wait_ge(S("tp_out"), tp_end(f"h_ffn{layer}"))
            for c in range(C):
                for k in range(DB):
                    last = nc.tensor.matmul(PS[:, 7, NE * c:NE * c + NE], HT[:, k, P * c:P * c + P], rw[:, k, :],
                                            start=k == 0, stop=k == DB - 1)
            last.then_inc(S("router_mm"), 1)
            pe.wait_ge(S("router_sig"), layer + 1)
            views = [slab_view(base + k, DB, DE) if k < 4 else slab_view(base + k, EB, D) for k in range(6)]
            with pe.Fori(0, NE // 2) as it:
                def loaded(k):
                    pe.wait_ge(S(f"slab{(base + k) % RING}"), it * 16 + 16 * ((base + k) // RING + 1))
                for j in range(2):
                    loaded(2 * j)
                    loaded(2 * j + 1)
                    for m in range(EB):
                        pe.wait_ge(S(f"act{layer}"), it * 8 + (4 * j + m + 1))
                        for x in range(2):
                            for k in range(DB):
                                last = nc.tensor.matmul(PS[:, m, T * x:T * x + T],
                                                        views[2 * j + x][:, k, P * m:P * m + P], HT[:, k, :],
                                                        start=k == 0, stop=k == DB - 1)
                        last.then_inc(S(f"gu_done{layer}"), 1)
                for j in range(2):
                    loaded(4 + j)
                    pe.wait_ge(S(f"act{layer}"), it * 8 + (4 * j + 8))
                    for i in range(4):
                        c, n = i // 2, i % 2
                        pe.wait_ge(S(f"y_done{layer}"), it * 8 + (4 * j + i + 1))
                        for k in range(EB):
                            last = nc.tensor.matmul(PS[:, 4 + i, :], AT[:, j, k, P * c:P * c + P],
                                                    views[4 + j][:, k, 512 * n:512 * n + 512],
                                                    start=k == 0, stop=k == EB - 1)
                        last.then_inc(S(f"down_done{layer}"), 1)

        pe.wait_ge(S("consts_in"), 16)
        gemm("mod0", None, ("c_act", 1))
        tp("h_a", ("h_ready", h_no["a"]))
        gemm("a_qk", HT, ht("h_a"))
        gemm("a_v", HT)
        pe.wait_ge(S("logf"), 1)
        for c in range(C):
            nc.tensor.matmul(PS[:, 0, HEADS * c:HEADS * c + HEADS], tri, F[:, c, :], start=True, stop=c == 0)
            if c:
                last = nc.tensor.matmul(PS[:, 0, HEADS * c:HEADS * c + HEADS], ones, F[:, 0, :],
                                        start=False, stop=True)
        last.then_inc(S("cum_mm"), 1)
        tp("cum", ("negcum", 1))
        attention("A", [ht("cum")])
        gemm("a_o", ATT["A"]["O"], ("oA", 8))
        tp("h_ffn0", ("h_ready", h_no["ffn0"]))
        experts(0)
        gemm("kvmod", None, ("x_ready", x_no["moe0"]))
        gemm("mod1", None)
        tp("h_kv", ("h_ready", h_no["kv"]))
        gemm("kv_down", HT, ht("h_kv"))
        tp("ckv", ("ckv", 1))
        gemm("kv_up", CKVT, ht("ckv"))
        tp("kB", ("krope", 1), evac_at[stages["kv_up"][-1][0]])
        tp("h_b", ("h_ready", h_no["b"]))
        gemm("b_dq", HT, ht("h_b"))
        tp("cq", ("cq", 1))
        gemm("b_uq", CQT, ht("cq"))
        tp("qB", ("qrope", 1))
        attention("B", [ht("qB")])
        gemm("b_o", ATT["B"]["O"], ("oB", 8))
        tp("h_ffn1", ("h_ready", h_no["ffn1"]))
        experts(1)
        tp("h_n1", ("h_ready", h_no["n1"]))
        gemm("c_u", HT, ht("h_n1"))
        gemm("c_p", HT)
        gemm("c_g", HT)
        tp("ssm_w", ("ssm_b", 1))
        tp("u", evac_at[stages["c_u"][-1][0]])
        pe.wait_ge(*(S("tp_out"), tp_end("u")))
        pe.wait_ge(S(evac_at[stages["c_g"][-1][0]][0]), evac_at[stages["c_g"][-1][0]][1])
        for b in range(4):
            if b:
                pe.wait_ge(S("bu_read"), b)
            for x in range(2):
                for i in range(4):
                    q = slice(32 * i, 32 * i + 32)
                    last = nc.tensor.matmul(PS[:, i, T * x:T * x + T], BT[x][q, b, :],
                                            UT[q, b, :], start=True, stop=True, tile_position=(32 * i, 0))
            last.then_inc(S("bu"), 1)
            pe.wait_ge(S("states"), b + 1)
            for i in range(4):
                for c in range(C):
                    o = PS[:, 6 + c, 32 * (4 * b + i):32 * (4 * b + i) + 32]
                    nc.tensor.matmul(o, Sr[:, i, P * c:P * c + P], CT[0][:, b, 32 * i:32 * i + 32],
                                     start=True, stop=False)
                    last = nc.tensor.matmul(o, Si[:, i, P * c:P * c + P], CT[1][:, b, 32 * i:32 * i + 32],
                                            start=False, stop=True)
            last.then_inc(S("y5_mm"), 1)
        tp("y5", ("y5", 1))
        gemm("glu", Y5T, ht("y5"))
        tp("y5g", ("y5g", 1))
        tp("qC", ("ropeC", 1))
        tp("kC")
        tp("qi")
        tp("ki")
        pe.wait_ge(S("tp_out"), tp_end("ki"))
        for c in range(C):
            if c:
                pe.wait_ge(S("index_read"), c)
            kl = P * (c + 1)
            for h in range(IH):
                q = slice(32 * (h % 4), 32 * (h % 4) + 32)
                last = nc.tensor.matmul(PS[:, h % 4, T * (h // 4):T * (h // 4) + kl],
                                        QIT[q, h // 4, P * c:P * c + P], KIT[q, 0:kl], start=True, stop=True,
                                        tile_position=(32 * (h % 4), 0))
            last.then_inc(S("index_mm"), 1)
        attention("C", [("index_read", 2)])
        gemm("ssm_up", Y5T, ("oC", 4))
        gemm("attn_up", ATT["C"]["O"])
        tp("merged", ("merged", 1))
        gemm("c_o", HT, ht("merged"))
        tp("peer_k", ("peerk_in", 32))
        tp("h_n2", ("h_ready", h_no["n2"]))
        gemm("peer_q", HT, ht("h_n2"))
        pe.wait_ge(S(evac_at[-1][0]), evac_at[-1][1])
        for c in range(C):
            for b in range(16):
                if b % 4 == 0 and c:
                    pe.wait_ge(S("peer_sc"), 4 * (c - 1) + b // 4 + 1)
                last = nc.tensor.matmul(PS[:, b // 4, P * (b % 4):P * (b % 4) + P], PQT[:, b, P * c:P * c + P],
                                        KT[:, b, :], start=True, stop=True)
                if b % 4 == 3:
                    last.then_inc(S("peer_mm"), 1)

    @block.scalar
    def _(act):
        A_ = nc.scalar.activation

        def tp(name):
            first, batches = TPJ[name]
            for b, (srcs, dst, scale) in enumerate(batches):
                n = first + b
                act.wait_ge(S("tp_done"), n + 1)
                w = srcs[0].shape[-1]
                A_(dst, PS[0:w, 4 + n % 4, 0:P * len(srcs)], ACT.Copy, scale=scale).then_inc(S("tp_out"), 1)

        def evac(name, fn, *waits):
            for w, n in waits:
                act.wait_ge(S(w), n)
            for i, (g, r, off, n, kind) in enumerate(stages[name]):
                act.wait_ge(S("gemm_done"), g + 1)
                fn(i, PS[:, 2 * (g % 2):2 * (g % 2) + 2, 0:n]).then_inc(S("evac_a"), 1)

        def to_rows(dst, at=0):
            def fn(i, banks, dst=dst):
                n = banks.shape[-1]
                return A_(dst[:, :, at + 512 * i:at + 512 * i + n], banks, ACT.Copy)
            return fn

        def attention(a):
            z = ATT[a]
            steps = [(g, c) for g in range(z["heads"] // 4) for c in range(C)]

            def exps(n):
                g, c = steps[n]
                act.wait_ge(S(f"negmax{a}"), n + 1)
                sc = z["SC"][:, n % 2, 0:4 * P * (c + 1)].rearrange("p (h k) -> p h k", h=4)
                for i in range(4):
                    last = A_(sc[:, i, :], sc[:, i, :], ACT.Exp, bias=st[:, 4 * (n % 2) + i:4 * (n % 2) + i + 1],
                              accum_out=st[:, 8 + 4 * (n % 2) + i:8 + 4 * (n % 2) + i + 1])
                last.then_inc(S(f"exp{a}"), 1)

            def pt(n):
                c = steps[n][1]
                act.wait_ge(S(f"ptp{a}"), n + 1)
                if n >= 2:
                    act.wait_ge(S(f"omm{a}"), n - 1)
                m = 512 * (c + 1)
                A_(z["PT"][:, n % 2, 0:m].rearrange("p (b k) -> p b k", k=512), PS[:, 4:4 + c + 1, :],
                   ACT.Copy).then_inc(S(f"pt{a}"), 1)

            def o(n):
                g, c = steps[n]
                act.wait_ge(S(f"omm{a}"), n + 1)
                A_(z["O"][:, 2 * g:2 * g + 2, P * c:P * c + P],
                   PS[:, 6 + n % 2, 0:2 * P].rearrange("p (a k) -> p a k", a=2), ACT.Copy).then_inc(S(f"o{a}"), 1)

            N = len(steps)
            for n in range(N + 2):
                if n < N:
                    exps(n)
                if 1 <= n <= N:
                    pt(n - 1)
                if n >= 2:
                    o(n - 2)

        def experts(layer):
            act.wait_ge(S("router_mm"), layer + 1)
            A_(RSC.rearrange("p c e -> p (c e)"), PS[:, 7, 0:C * NE], ACT.Sigmoid).then_inc(S("router_sig"), 1)
            with act.Fori(0, NE // 2) as it:
                for q in range(8):
                    act.wait_ge(S(f"gu_done{layer}"), it * 8 + (q + 1))
                    act.wait_ge(S(f"act{layer}"), it * 8 + (q + 1))
                    A_(SG[:, q % 4, :], PS[:, q % 4, 0:T], ACT.Silu).then_inc(S(f"silu{layer}"), 1)

        act.wait_ge(S("c_in"), 16)
        A_(cT[:, :], cT[:, :], ACT.Silu).then_inc(S("c_act"), 1)
        act.wait_ge(S("ang"), 1)
        A_(rope_cs[:, 1, :, :], rope_cs[:, 0, :, :], ACT.Sin)
        A_(rope_cs[:, 0, :, :], rope_cs[:, 0, :, :], ACT.Sin, scale=0.5).then_inc(S("sin"), 1)
        tp("h_a")
        z = ATT["A"]

        def qk_out(i, banks):
            dst = (z["Q"] if i < 2 else z["K"])[:, 4 * (i % 2):4 * (i % 2) + 4, :]
            return A_(dst.rearrange("p (u a) t -> p u (a t)", u=2), banks, ACT.Copy, scale=0.125 if i < 2 else 1.0)
        evac("a_qk", qk_out)
        evac("a_v", lambda i, banks: to_rows(z["V"])(i, banks) if i < 2 else A_(F, banks, ACT.Copy))
        act.wait_ge(S("f_abs"), 1)
        A_(Ft, Ft, ACT.Exp, scale=-1.0).then_inc(S("f_exp"), 1)
        act.wait_ge(S("f_exp"), 1)
        A_(Ft, Ft, ACT.Ln, bias=ones[:, 0:1]).then_inc(S("f_ln"), 1)
        act.wait_ge(S("cum_mm"), 1)
        A_(Fn, PS[:, 0, 0:C * HEADS].rearrange("p (c h) -> p c h", c=C), ACT.Copy, scale=-1.0).then_inc(S("negcum"), 1)
        tp("cum")
        attention("A")
        evac("a_o", to_rows(H))
        tp("h_ffn0")
        experts(0)
        tp("h_kv")
        evac("kv_down", lambda i, banks: A_(CKV, banks, ACT.Copy))
        tp("ckv")

        def kv_out(i, banks):
            b = banks.rearrange("p c (h d) -> p c h d", h=4)
            for c in range(C):
                A_(KTOK[:, c, 4 * i:4 * i + 4, 0:NOPE], b[:, c, :, 0:NOPE], ACT.Copy)
            return A_(ATT["B"]["V"][:, :, 256 * i:256 * i + 256].rearrange("p c (h d) -> p c h d", h=4),
                      b[:, :, :, NOPE:P], ACT.Copy)
        evac("kv_up", kv_out)
        tp("kB")
        tp("h_b")
        evac("b_dq", to_rows(CQ))
        tp("cq")
        evac("b_uq", to_rows(QTOK.rearrange(flat)))
        tp("qB")
        attention("B")
        evac("b_o", to_rows(H))
        tp("h_ffn1")
        experts(1)
        act.wait_ge(S("ssm_in"), 16 * (2 * 2 + 8 * 2 + 6))
        A_(SP_[2], SP_[2], ACT.Exp).then_inc(S("dt"), 1)
        tp("h_n1")
        evac("c_u", to_rows(U))
        act.wait_ge(S("ssm_ang"), 1)
        A_(SP_[6], SP_[3], ACT.Exp)
        A_(SP_[7], SP_[5], ACT.Sin)
        A_(SP_[8], SP_[5], ACT.Sin, scale=0.5).then_inc(S("ssm_sin"), 1)
        evac("c_p", to_rows(PROJ))
        evac("c_g", lambda i, banks: A_(GATES[:, :, 512 * i:512 * i + 512], banks, ACT.Sigmoid))
        tp("ssm_w")
        tp("u")
        act.wait_ge(S("y5_pre"), 1)
        A_(Y5, Y5, ACT.Gelu_apprx_tanh).then_inc(S("y5"), 1)
        tp("y5")
        evac("glu", lambda i, banks: A_(U, banks, ACT.Sigmoid))
        tp("y5g")
        tp("qC")
        tp("kC")
        tp("qi")
        tp("ki")
        attention("C")
        evac("ssm_up", to_rows(M1))
        evac("attn_up", to_rows(M2))
        tp("merged")
        evac("c_o", to_rows(M2))
        tp("peer_k")
        tp("h_n2")
        evac("peer_q", lambda i, banks: A_(PQT[:, 4 * i:4 * i + 4, :].rearrange("p (u a) t -> p u (a t)", u=2), banks,
                                           ACT.Copy))
        for c in range(C):
            for q in range(4):
                act.wait_ge(S("peer_mm"), 4 * c + q + 1)
                if c and q == 0:
                    act.wait_ge(S("peer_top"), 1)
                A_(PSC[:, 4 * q:4 * q + 4, :].rearrange("p a k -> p (a k)"), PS[:, q, :], ACT.Copy
                   ).then_inc(S("peer_sc"), 1)
            act.wait_ge(S("top_shift"), c + 1)
            A_(TV, TV, ACT.Exp).then_inc(S("top_exp"), 1)
        for half in range(2):
            act.wait_ge(S(f"rows_used{half}"), 2 * (SEL // 16) + 1)
        A_(DOT, DOT, ACT.Gelu_apprx_tanh).then_inc(S("gelu"), 1)

    @block.vector
    def _(dve):
        V = nc.vector

        def L(ins):
            link(dve, ins, "v")

        def tt(o, a, b, op):
            L(V.tensor_tensor(o, a, b, op))

        def ts(o, a, s1, op0, s2=None, op1=None):
            if op1 is None:
                L(V.tensor_scalar(o, a, s1, None, op0))
            else:
                L(V.tensor_scalar(o, a, s1, s2, op0, op1))

        def wait(name, n):
            dve.wait_ge(S(name), n)

        def inverse_root(y, v, t):
            L(V.tensor_single_scalar(t.bitcast(i32), v.bitcast(i32), 1, ALU.logical_shift_right))
            ts(y.bitcast(i32), t.bitcast(i32), -1.0, ALU.mult, float(0x5F3759DF), ALU.add)
            for _ in range(4):
                tt(t, y, y, ALU.mult)
                tt(t, t, v, ALU.mult)
                ts(t, t, -0.5, ALU.mult, 1.5, ALU.add)
                tt(y, y, t, ALU.mult)

        def rms(src, width, dst, gname, junk=None, signal=None):
            wait("gain_in", 16 * (gain_no[gname] + 1))
            junk = dst if junk is None else junk
            V.scalar_tensor_tensor(junk[:, 0, 0:width], src[:, 0, :], 1.0, src[:, 0, :], ALU.mult, ALU.mult,
                                   accum_out=st[:, 0:1])
            L(V.scalar_tensor_tensor(junk[:, 1, 0:width], src[:, 1, :], 1.0, src[:, 1, :], ALU.mult, ALU.mult,
                                     accum_out=st[:, 1:2]))
            ts(st[:, 2:4], st[:, 0:2], 1.0 / width, ALU.mult, EPS, ALU.add)
            inverse_root(st[:, 4:6], st[:, 2:4], st[:, 6:8])
            for c in range(C):
                last = V.scalar_tensor_tensor(dst[:, c, :], src[:, c, :], st[:, 4 + c:5 + c],
                                              GAIN[:, 0:width], ALU.mult, ALU.mult)
                if c == 0:
                    L(last)
            last.then_inc(S("gain_used"), 1)
            wait("gain_used", gain_no[gname] + 1)
            if signal:
                V.tensor_copy(st[:, 9:10], st[:, 8:9]).then_inc(S(signal), 1)

        def modulate(shift, scale):
            for c in range(C):
                L(V.scalar_tensor_tensor(H[:, c, :], scale, 1.0, H[:, c, :], ALU.add, ALU.mult))
            for c in range(C):
                last = V.tensor_tensor(H[:, c, :], H[:, c, :], shift, ALU.add)
                if c == 0:
                    L(last)
            last.then_inc(S("h_ready"), 1)

        def mod_part(i):
            return MOD[:, D * i:D * (i + 1)]

        def add_bias(name, dst):
            for i, (g, r, off, n, kind) in enumerate(stages[name]):
                wait("gemm_done", g + 1)
                V.tensor_tensor(dst[:, 512 * i:512 * i + n], PS[:, 2 * (g % 2), 0:n], dst[:, 512 * i:512 * i + n],
                                ALU.add).then_inc(S("evac_v"), 1)
            wait("evac_v", evac_at[stages[name][-1][0]][1])

        def wait_evac(name):
            e = evac_at[stages[name][-1][0]]
            wait(*e)

        def gated_add(y, gate, ready):
            if gate is not None:
                for c in range(C):
                    L(V.tensor_tensor(y[:, c, :], y[:, c, :], gate, ALU.mult))
            V.tensor_tensor(X[:, :, :], X[:, :, :], y, ALU.add).then_inc(S("x_ready"), 1)
            wait("x_ready", x_no[ready])

        def reduce_angle(a, t):
            ts(t, a, 1.0 / (2 * math.pi), ALU.mult)
            ts(t, t, ROUND, ALU.add)
            ts(t, t, ROUND, ALU.subtract)
            for k in (TWO_PI_A, TWO_PI_B, TWO_PI_C):
                L(V.scalar_tensor_tensor(a, t, -k, a, ALU.mult, ALU.add))
            ts(a, a, PI, ALU.min, -PI, ALU.max)

        def rope(x1, x2, cos, sin, t):
            tt(t[0], x1, cos, ALU.mult)
            tt(t[1], x2, sin, ALU.mult)
            tt(t[2], x2, cos, ALU.mult)
            tt(t[3], x1, sin, ALU.mult)
            tt(x1, t[0], t[1], ALU.subtract)
            tt(x2, t[2], t[3], ALU.add)

        def attention(a):
            z = ATT[a]
            steps = [(g, c) for g in range(z["heads"] // 4) for c in range(C)]

            def mask(n):
                g, c = steps[n]
                kl = P * (c + 1)
                wait(f"scores{a}", n + 1)
                if n >= 2:
                    wait(f"ptp{a}", n - 1)
                sc = z["SC"][:, n % 2, 0:4 * kl].rearrange("p (h k) -> p h k", h=4)
                ps = PS[:, 2 * (n % 2):2 * (n % 2) + 2, :].rearrange("p b (x k) -> p (b x) k", x=2)[:, :, 0:kl]
                if z["mask"] is None:
                    m, op = MASKC[:, c, 0:kl], ALU.add
                else:
                    m, op = consts[:, z["mask"] + P * c:z["mask"] + P * c + kl], ALU.min
                V.scalar_tensor_tensor(sc, ps, z["scale"],
                                       m.rearrange("p (a k) -> p a k", a=1).to_broadcast((P, 4, kl)), ALU.mult, op
                                       ).then_inc(S(f"masked{a}"), 1)
                wait(f"masked{a}", n + 1)
                V.tensor_reduce(st[:, 4 * (n % 2):4 * (n % 2) + 4], sc, AX.X, ALU.max, negate=True
                                ).then_inc(S(f"negmax{a}"), 1)

            def norm(n):
                g, c = steps[n]
                kl = P * (c + 1)
                wait(f"exp{a}", n + 1)
                r = st[:, 8 + 4 * (n % 2):12 + 4 * (n % 2)]
                L(V.reciprocal(r, r))
                sc = z["SC"][:, n % 2, 0:4 * kl].rearrange("p (h k) -> p h k", h=4)
                V.tensor_tensor(sc, sc, r.rearrange("p (h a) -> p h a", a=1).to_broadcast((P, 4, kl)), ALU.mult
                                ).then_inc(S(f"probs{a}"), 1)

            mask(0)
            for n in range(len(steps)):
                if n + 1 < len(steps):
                    mask(n + 1)
                norm(n)
            wait(f"probs{a}", len(steps))

        def experts(layer):
            wait("router_sig", layer + 1)
            tt(RSEL, RSC, rb[:, :].rearrange("p (a e) -> p a e", a=1).to_broadcast((P, C, NE)), ALU.add)
            q = RSEL.rearrange("p c (g e) -> p c g e", e=EPG)
            def tmp(i, n=C * NG):
                return RT[:, 32 * i:32 * i + n]
            def g4(i):
                return tmp(i).rearrange("p (c g) -> p c g", c=C)
            tt(g4(0), q[:, :, :, 0], q[:, :, :, 1], ALU.max)
            tt(g4(1), q[:, :, :, 0], q[:, :, :, 1], ALU.min)
            tt(g4(2), q[:, :, :, 2], q[:, :, :, 3], ALU.max)
            tt(g4(3), q[:, :, :, 2], q[:, :, :, 3], ALU.min)
            tt(g4(4), g4(0), g4(2), ALU.max)
            tt(g4(5), g4(0), g4(2), ALU.min)
            tt(g4(1), g4(1), g4(3), ALU.max)
            tt(g4(5), g4(5), g4(1), ALU.max)
            tt(g4(4), g4(4), g4(5), ALU.add)
            best = RT[:, 192:194]
            L(V.tensor_reduce(best, g4(4), AX.X, ALU.max))
            tt(g4(0), g4(4), best.rearrange("p (c a) -> p c a", a=1).to_broadcast((P, C, NG)), ALU.is_equal)
            for c in range(C):
                L(V.tensor_tensor_scan(g4(1)[:, c, :], ones[:, 0:NG], g4(0)[:, c, :], 0.0, ALU.mult, ALU.add))
            L(V.scalar_tensor_tensor(g4(0), g4(1), 1.0, g4(0), ALU.is_equal, ALU.mult))
            ts(g4(1), g4(0), 1.0, ALU.subtract, -NEG, ALU.mult)
            for c in range(C):
                qc = RSEL[:, c, :].rearrange("p (g e) -> p g e", e=EPG)
                tt(qc, qc, g4(1)[:, c, :].rearrange("p (g a) -> p g a", a=1).to_broadcast((P, NG, EPG)), ALU.add)
            top8 = RT[:, 200:216].rearrange("p (c k) -> p c k", c=C)
            idx = RT[:, 216:232].rearrange("p (c k) -> p c k", c=C)
            for c in range(C):
                L(V.max(top8[:, c, :], RSEL[:, c, :]))
                L(V.max_index(RIDX[:, c, :], top8[:, c, :], RSEL[:, c, :]))
            L(V.tensor_copy(idx, RIDX))
            oh = [RT[:, 256 + 32 * i:288 + 32 * i].rearrange("p (c e) -> p c e", c=C) for i in range(2)]
            iota = consts[:, K_IOTA:K_IOTA + NE].rearrange("p (a e) -> p a e", a=1).to_broadcast((P, C, NE))
            for i in range(2):
                tt(oh[i], iota, idx[:, :, i:i + 1].to_broadcast((P, C, NE)), ALU.is_equal)
            tt(oh[0], oh[0], oh[1], ALU.add)
            tt(COMB, oh[0], RSC, ALU.mult)
            L(V.tensor_reduce(best, COMB, AX.X, ALU.add))
            L(V.reciprocal(best, best))
            tt(COMB, COMB, best.rearrange("p (c a) -> p c a", a=1).to_broadcast((P, C, NE)), ALU.mult)
            L(V.memset(Y, 0.0))
            dve.sem_inc(S(f"y_done{layer}"), 4)
            with dve.Fori(0, NE // 2) as it:
                for j in range(2):
                    wait(f"down_done{layer}", it * 8 + (4 * j + 4))
                    for m in range(EB):
                        wait(f"silu{layer}", it * 8 + (4 * j + m + 1))
                        V.tensor_tensor(AT[:, j, m, :], SG[:, m, :], PS[:, m, T:2 * T], ALU.mult
                                        ).then_inc(S(f"act{layer}"), 1)
                for j in range(2):
                    for i in range(4):
                        c, n = i // 2, i % 2
                        wait(f"down_done{layer}", it * 8 + (4 * j + i + 1 + 8))
                        y = Y[:, c, 512 * n:512 * n + 512]
                        wait(f"y_done{layer}", it * 8 + (4 * j + i + 1))
                        V.scalar_tensor_tensor(y, PS[:, 4 + i, :], COMB[:, c, bass.ds(it * 2 + j, 1)], y,
                                               ALU.mult, ALU.add).then_inc(S(f"y_done{layer}"), 1)
            wait(f"y_done{layer}", 4 * NE + 4)

        for layer in range(2):
            dve.sem_inc(S(f"act{layer}"), 4)
            dve.sem_inc(S(f"down_done{layer}"), 8)
        wait("small_in", 64)
        wait("consts_in", 16)
        L(V.memset(st[:, :], 0.0))
        posf = st[:, 14:16]
        L(V.tensor_copy(posf, pos_i[:, :]))
        RA, RB_ = rope_cs[:, 0, :, :], rope_cs[:, 1, :, :]
        tt(RA, posf.rearrange("p (c a) -> p c a", a=1).to_broadcast((P, C, 16)),
           consts[:, K_INV:K_INV + 16].rearrange("p (a k) -> p a k", a=1).to_broadcast((P, C, 16)), ALU.mult)
        reduce_angle(RA, RB_)
        V.tensor_copy(st[:, 13:14], st[:, 14:15]).then_inc(S("ang"), 1)
        wait("sin", 1)
        tt(RA, RA, RA, ALU.mult)
        ts(RA, RA, -2.0, ALU.mult, 1.0, ALU.add)
        wait("modb_in", 16)
        add_bias("mod0", MOD)
        wait("x_in", 16)
        rms(X, D, H, "a")
        modulate(mod_part(0), mod_part(1))
        wait_evac("a_v")
        tt(F, F, bf[:, :].rearrange("p (a h) -> p a h", a=1).to_broadcast((P, C, HEADS)), ALU.add)
        V.scalar_tensor_tensor(Ft, F, -1.0, F, ALU.mult, ALU.max).then_inc(S("f_abs"), 1)
        ts(F, F, 0.0, ALU.min)
        wait("f_ln", 1)
        V.tensor_tensor(F, F, Ft, ALU.subtract).then_inc(S("logf"), 1)
        attention("A")
        wait_evac("a_o")
        gated_add(H, mod_part(2), "a_o")
        rms(X, D, H, "ffn0")
        modulate(mod_part(3), mod_part(4))
        experts(0)
        gated_add(Y, mod_part(5), "moe0")
        wait("kvb_in", 16)
        add_bias("kvmod", KM)
        rms(X, D, H, "kv")
        modulate(KM[:, 0:D], KM[:, D:2 * D])
        wait("modb_in", 32)
        add_bias("mod1", MOD)
        wait_evac("kv_down")
        heads = "p (a h) -> p a h"
        for c in range(C):
            rt = [view(HTm, 16 * i, 16) for i in range(4)]
            rope(CKV[:, c, KVR:KVR + 16], CKV[:, c, KVR + 16:KVR + 32], rope_cs[:, 0, c, :], rope_cs[:, 1, c, :], rt)
        for c in range(C):
            last = V.tensor_copy(KTOK[:, c, :, NOPE:QK],
                                 CKV[:, c, KVR:KVR + 32].rearrange("p (a r) -> p a r", a=1).to_broadcast((P, HEADS, ROPE)))
            if c == 0:
                L(last)
        last.then_inc(S("krope"), 1)
        rms(CKV[:, :, 0:KVR], KVR, CKV[:, :, 0:KVR], "latent", junk=HTm[:, 0:512].rearrange("p (c d) -> p c d", c=C),
            signal="ckv")
        wait("tp_out", tp_end("h_kv"))
        rms(X, D, H, "b")
        modulate(mod_part(0), mod_part(1))
        wait_evac("b_dq")
        rms(CQ, QR, CQ, "q", junk=HTm[:, 0:2 * QR].rearrange("p (c d) -> p c d", c=C), signal="cq")
        wait_evac("b_uq")
        for c in range(C):
            rt = [view(HTm, 256 * i, HEADS, 16) for i in range(4)]
            cs = [rope_cs[:, k, c, :].rearrange("p (a r) -> p a r", a=1).to_broadcast((P, HEADS, 16)) for k in range(2)]
            rope(QTOK[:, c, :, NOPE:NOPE + 16], QTOK[:, c, :, NOPE + 16:QK], cs[0], cs[1], rt)
        V.tensor_copy(st[:, 9:10], st[:, 8:9]).then_inc(S("qrope"), 1)
        wait("tp_out", tp_end("qB"))
        attention("B")
        wait_evac("b_o")
        gated_add(H, mod_part(2), "b_o")
        rms(X, D, H, "ffn1")
        modulate(mod_part(3), mod_part(4))
        experts(1)
        gated_add(Y, mod_part(5), "moe1")
        rms(X, D, X, "final", junk=H, signal="x_ready")
        rms(X, D, H, "n1", signal="h_ready")
        lr, li, dt, x, t, ang, ex, sn, sh, xc, p_, m_, em, cm, r_, ar_, ai_, dd, fr, fi, er, u_ = SP_[:22]
        wait("dt", 1)
        tt(x, lr, dt, ALU.mult)
        tt(ang, li, dt, ALU.mult)
        reduce_angle(ang, t)
        V.tensor_copy(st[:, 9:10], st[:, 8:9]).then_inc(S("ssm_ang"), 1)
        ts(xc, x, 0.5, ALU.min, -0.5, ALU.max)
        ts(p_, xc, 1.0 / 8, ALU.mult, 1.0, ALU.add)
        for k in (7, 6, 5, 4, 3, 2):
            tt(p_, p_, xc, ALU.mult)
            ts(p_, p_, 1.0 / k, ALU.mult, 1.0, ALU.add)
        tt(p_, p_, xc, ALU.mult)
        L(V.scalar_tensor_tensor(m_, x, -1.0, x, ALU.mult, ALU.max))
        ts(m_, m_, 0.5, ALU.is_lt)
        wait("ssm_sin", 1)
        ts(ex, ex, BIG, ALU.min, -1.0, ALU.add)
        tt(em, p_, ex, ALU.subtract)
        tt(em, em, m_, ALU.mult)
        tt(em, em, ex, ALU.add)
        tt(cm, sh, sh, ALU.mult)
        ts(cm, cm, -2.0, ALU.mult)
        ts(r_, em, 1.0, ALU.add)
        tt(ar_, r_, cm, ALU.mult)
        tt(ar_, ar_, em, ALU.add)
        tt(ai_, r_, sn, ALU.mult)
        tt(dd, lr, lr, ALU.mult)
        tt(t, li, li, ALU.mult)
        tt(dd, dd, t, ALU.add)
        L(V.reciprocal(dd, dd))
        for o, a1, b1, a2, b2, op in ((fr, ar_, lr, ai_, li, ALU.add), (fi, ai_, lr, ar_, li, ALU.subtract)):
            tt(o, a1, b1, ALU.mult)
            tt(t, a2, b2, ALU.mult)
            tt(o, o, t, op)
            tt(o, o, dd, ALU.mult)
        ts(er, cm, 1.0, ALU.add)
        frb, fib = (f.rearrange("p (t a) -> p t a", a=1).to_broadcast((P, ST, 32)) for f in (fr, fi))
        w4 = [ar(10320 + 512 * i, ST, 32) for i in range(4)]
        tt(w4[0], BN[0], frb, ALU.mult)
        tt(w4[1], BN[1], fib, ALU.mult)
        tt(w4[2], BN[1], frb, ALU.mult)
        tt(w4[3], BN[0], fib, ALU.mult)
        tt(BN[0], w4[0], w4[1], ALU.subtract)
        V.tensor_tensor(BN[1], w4[2], w4[3], ALU.add).then_inc(S("ssm_b"), 1)
        POW = [[ar(12752 + 32 * k + 16 * x_, ST) for x_ in range(2)] for k in range(8)]
        L(V.tensor_copy(POW[0][0], er))
        L(V.tensor_copy(POW[0][1], sn))
        for k in range(7):
            (a_, b_), (a2_, b2_) = POW[k], POW[k + 1]
            tt(a2_, a_, a_, ALU.mult)
            tt(t, b_, b_, ALU.mult)
            tt(a2_, a2_, t, ALU.subtract)
            tt(t, a_, b_, ALU.mult)
            ts(b2_, t, 2.0, ALU.mult)
        wait_evac("c_p")
        for c in range(C):
            for at, n, h, kc_, ks_ in ((0, 10, 32, K_COS64, K_SIN64), (768, 9, 16, K_COS32, K_SIN32)):
                v = PROJ[:, c, at:at + 2 * h * n].rearrange("p (n d) -> p n d", n=n)
                cs = [consts[:, k + h * c:k + h * c + h].rearrange("p (a r) -> p a r", a=1).to_broadcast((P, n, h))
                      for k in (kc_, ks_)]
                rope(v[:, :, 0:h], v[:, :, h:2 * h], cs[0], cs[1], [ar(10320 + 512 * i, n, h) for i in range(4)])
        wait("tp_out", tp_end("ssm_w"))
        wait("tp_out", tp_end("h_n1"))
        for b in range(4):
            q = slice(4 * b, 4 * b + 4)
            L(V.memset(Er[:, :, 0:1], 1.0))
            L(V.memset(Ei[:, :, 0:1], 0.0))
            for k in range(8):
                n = 1 << k
                pr, pi_ = (POW[k][x_][:, q].rearrange("p (t a) -> p t a", a=1).to_broadcast((P, 4, n)) for x_ in range(2))
                V.tensor_tensor(T1[:, :, 0:n], Er[:, :, 0:n], pr, ALU.mult)
                V.tensor_tensor(T2[:, :, 0:n], Ei[:, :, 0:n], pi_, ALU.mult)
                V.tensor_tensor(Zr[:, :, 0:n], Er[:, :, 0:n], pi_, ALU.mult)
                tt(Zi[:, :, 0:n], Ei[:, :, 0:n], pr, ALU.mult)
                V.tensor_tensor(Er[:, :, n:2 * n], T1[:, :, 0:n], T2[:, :, 0:n], ALU.subtract)
                tt(Ei[:, :, n:2 * n], Zr[:, :, 0:n], Zi[:, :, 0:n], ALU.add)
            wait("bu", b + 1)
            br, bi = (PS[:, 0:4, T * x_:T * x_ + T] for x_ in range(2))
            V.tensor_tensor(T1, br, Er, ALU.mult)
            V.tensor_tensor(T2, bi, Ei, ALU.mult)
            V.tensor_tensor(Zr, bi, Er, ALU.mult)
            V.tensor_tensor(Zi, br, Ei, ALU.mult).then_inc(S("bu_read"), 1)
            wait("bu_read", b + 1)
            tt(T1, T1, T2, ALU.add)
            tt(T2, Zr, Zi, ALU.subtract)
            for i in range(4):
                rr = r_[:, 4 * b + i:4 * b + i + 1].to_broadcast((P, T))
                V.tensor_tensor_scan(Zr[:, i, :], rr, T1[:, i, :], 0.0, ALU.mult, ALU.add)
                last = V.tensor_tensor_scan(Zi[:, i, :], rr, T2[:, i, :], 0.0, ALU.mult, ALU.add)
            L(last)
            V.tensor_tensor(T1, Zr, Er, ALU.mult)
            tt(T2, Zi, Ei, ALU.mult)
            if b:
                wait("y5_mm", b)
            tt(Sr, T1, T2, ALU.subtract)
            V.tensor_tensor(T1, Zr, Ei, ALU.mult)
            tt(T2, Zi, Er, ALU.mult)
            V.tensor_tensor(Si, T1, T2, ALU.add).then_inc(S("states"), 1)
            wait("states", b + 1)
        wait("gain_in", 16 * (gain_no["dskip"] + 1))
        V.tensor_tensor(Y5, U, GAIN[:, 0:SSM_W].rearrange("p (a d) -> p a d", a=1).to_broadcast((P, C, SSM_W)), ALU.mult
                        ).then_inc(S("gain_used"), 1)
        wait("gain_used", gain_no["dskip"] + 1)
        wait("y5_mm", 4)
        V.tensor_tensor(Y5, Y5, PS[:, 6:8, :], ALU.add).then_inc(S("y5_pre"), 1)
        wait_evac("glu")
        V.tensor_tensor(Y5, Y5, U, ALU.mult).then_inc(S("y5g"), 1)
        for c in range(C):
            L(V.tensor_copy(KD[:, c, :, :, :], PROJ[:, c, 512:640].rearrange("p (k a d) -> p k a d", k=2, a=1)
                            .to_broadcast((P, 2, 2, HD))))
            last = V.tensor_copy(KI4[:, c, :, :], PROJ[:, c, 1024:1056].rearrange("p (a d) -> p a d", a=1)
                                 .to_broadcast((P, 4, ID)))
            if c == 0:
                L(last)
        last.then_inc(S("ropeC"), 1)
        wait("tp_out", tp_end("ki"))
        for c in range(C):
            kl = P * (c + 1)
            wait("index_mm", c + 1)
            ps = PS[:, 0:4, :].rearrange("p b (x k) -> p (b x) k", x=2)[:, :, 0:kl]
            L(V.tensor_copy(WI.rearrange("p (b x) -> p b x", x=2), PROJ[:, c, 1056:1064].rearrange("p (x b) -> p b x", x=2)))
            V.scalar_tensor_tensor(RELU[:, :, 0:kl], ps, 0.0,
                                   WI.rearrange("p (h a) -> p h a", a=1).to_broadcast((P, IH, kl)),
                                   ALU.max, ALU.mult).then_inc(S("index_read"), 1)
            wait("index_read", c + 1)
            sc, left = SCORE[:, 0:kl], SLEFT[:, 0:kl]
            clamp = consts[:, K_CAUSAL + P * c:K_CAUSAL + P * c + kl]
            L(V.tensor_reduce(sc, RELU[:, :, 0:kl].rearrange("p h k -> p k h"), AX.X, ALU.add))
            L(V.scalar_tensor_tensor(sc, sc, (IH * ID) ** -0.5, clamp, ALU.mult, ALU.min))
            for k in range(TOPK // 8):
                L(V.max(T8, left if k else sc))
                L(V.match_replace(left, T8, left if k else sc, -BIG))
            tt(MASKC[:, c, 0:kl], left, sc, ALU.is_equal)
            L(V.scalar_tensor_tensor(MASKC[:, c, 0:kl], MASKC[:, c, 0:kl], NEG, clamp, ALU.mult, ALU.min))
        attention("C")
        wait_evac("attn_up")
        V.tensor_tensor(M1, M1, GATES[:, :, 0:D], ALU.mult)
        tt(M2, M2, GATES[:, :, D:2 * D], ALU.mult)
        V.tensor_tensor(M1, M1, M2, ALU.add).then_inc(S("merged"), 1)
        wait_evac("c_o")
        gated_add(M2, None, "c_o")
        rms(X, D, H, "n2", signal="h_ready")
        for half in range(2):
            dve.sem_inc(S(f"rows_used{half}"), 1)
            dve.sem_inc(S(f"x_acc{half}"), 1)
        iota = consts[:, K_IOTA:K_IOTA + PT_].rearrange("p (a e) -> p a e", a=1).to_broadcast((P, SEL, PT_))
        for c in range(C):
            for b in range(16):
                if b % 4 == 0:
                    wait("peer_sc", 4 * c + b // 4 + 1)
                for k in range(2):
                    v8, i8 = V16[:, b, 8 * k:8 * k + 8], I16[:, b, 8 * k:8 * k + 8]
                    L(V.max(v8, PSC[:, b, :]))
                    last = V.max_index(i8, v8, PSC[:, b, :])
                    if k == 0:
                        L(last)
                        L(V.match_replace(PSC[:, b, :], v8, PSC[:, b, :], -BIG))
            last.then_inc(S("peer_top"), 1)
            wait("peer_top", c + 1)
            V.tensor_copy(I16F, I16)
            for h in range(PH):
                last = V.tensor_tensor(CAND[:, h, :].rearrange("p (i j) -> p i j", i=PT_),
                                       V16[:, 2 * h, :].rearrange("p (i a) -> p i a", a=1).to_broadcast((P, PT_, PT_)),
                                       V16[:, 2 * h + 1, :].rearrange("p (a j) -> p a j", a=1).to_broadcast((P, PT_, PT_)),
                                       ALU.add)
            L(last)
            for h in range(PH):
                for k in range(2):
                    v8, i8 = TV[:, h, 8 * k:8 * k + 8], TP_[:, h, 8 * k:8 * k + 8]
                    L(V.max(v8, CAND[:, h, :]))
                    L(V.max_index(i8, v8, CAND[:, h, :]))
                    if k == 0:
                        L(V.match_replace(CAND[:, h, :], v8, CAND[:, h, :], -BIG))
            V.tensor_single_scalar(HI, TP_.rearrange("p h k -> p (h k)"), 4, ALU.logical_shift_right)
            L(V.tensor_single_scalar(LO, TP_.rearrange("p h k -> p (h k)"), 15, ALU.bitwise_and))
            V.tensor_copy(HIF, HI)
            L(V.tensor_copy(LOF, LO))
            for half, (pos, o) in enumerate(((HIF, EHI), (LOF, ELO))):
                tt(PTMP, iota, pos.rearrange("p (s a) -> p s a", a=1).to_broadcast((P, SEL, PT_)), ALU.is_equal)
                for h in range(PH):
                    last = V.tensor_tensor(PTMP[:, 16 * h:16 * h + 16, :], PTMP[:, 16 * h:16 * h + 16, :],
                                           I16F[:, 2 * h + half, :].rearrange("p (a e) -> p a e", a=1)
                                           .to_broadcast((P, PT_, PT_)), ALU.mult)
                L(last)
                L(V.tensor_reduce(o, PTMP, AX.X, ALU.add))
            V.scalar_tensor_tensor(EXPERT[:, c, :], EHI, float(PK), ELO, ALU.mult, ALU.add).then_inc(S("experts"), 1)
            L(V.tensor_copy(PSUMS, TV[:, :, 0]))
            V.tensor_tensor(TV, TV, PSUMS.rearrange("p (h a) -> p h a", a=1).to_broadcast((P, PH, PT_)), ALU.subtract
                            ).then_inc(S("top_shift"), 1)
            wait("top_exp", c + 1)
            L(V.tensor_reduce(PSUMS, TV, AX.X, ALU.add))
            L(V.reciprocal(PSUMS, PSUMS))
            tt(GATE[:, c, :].rearrange("p (h k) -> p h k", h=PH), TV,
               PSUMS.rearrange("p (h a) -> p h a", a=1).to_broadcast((P, PH, PT_)), ALU.mult)
        def rows(half, j):
            return ring[:, (8 * half + j) * D:(8 * half + j + 1) * D]

        for c in range(C):
            with dve.Fori(0, SEL // 16) as i:
                for half in range(2):
                    wait(f"rows_in{half}", i * P + P * (8 * c + 1))
                    for j in range(8):
                        last = V.scalar_tensor_tensor(rows(half, j), rows(half, j), 1.0, H[:, c, :], ALU.mult, ALU.mult,
                                                      accum_out=DOT[:, c, bass.ds(i * 16 + 8 * half + j, 1)])
                    last.then_inc(S(f"rows_used{half}"), 1)
        wait("gelu", 1)
        tt(DOT, DOT, GATE, ALU.mult)
        for c in range(C):
            with dve.Fori(0, SEL // 16) as i:
                for half in range(2):
                    wait(f"rows_in{half}", i * P + P * (16 + 8 * c + 1))
                    for j in range(8):
                        n = 8 * half + j
                        V.scalar_tensor_tensor(X[:, c, :], rows(half, j), DOT[:, c, bass.ds(i * 16 + n, 1)], X[:, c, :],
                                               ALU.mult, ALU.add).then_inc(S(f"x_acc{half}"), 1)
                        wait(f"x_acc{half}", i * 8 + (64 * c + j + 2))
        rms(X, D, H, "nf", signal="result")

    return ctx


INPUTS = ["x", "c", "positions", "a_norm_g", "a_w_in", "a_b_f", "a_w_o", "kv_norm_g", "kv_w_mod", "kv_b_mod",
          "kv_w_down", "kv_latent_g", "kv_w_up", "b_norm_g", "b_w_dq", "b_q_norm_g", "b_w_uq", "b_w_o", "w_mod",
          "b_mod", "ffn_norm_g", "router_w", "router_bias", "exp_w_gate", "exp_w_up", "exp_w_down", "final_norm_g",
          "norm1_g_2", "w_in_2", "a_re_2", "a_im_2", "log_dt_2", "b_re_2", "b_im_2", "c_re_2", "c_im_2", "d_skip_2",
          "w_glu_2", "w_ssm_up_2", "w_attn_up_2", "w_out_2", "norm2_g_2", "peer_wq_2", "peer_k1_2", "peer_k2_2",
          "peer_u_2", "peer_v_2", "norm_f_g_2"]


def kernel(**inputs):
    import concourse.bacc as bacc
    from concourse.bass_utils import run_bass_kernel_spmd

    nc = bacc.Bacc("TRN2", target_bir_lowering=False, num_devices=1)
    arrays, args = {}, {}
    given = {name: np.ascontiguousarray(inputs[name]) for name in INPUTS}
    given["consts"] = shape_constants()
    for name, a in given.items():
        arrays[f"in_{name}"] = a
        args[name] = nc.dram_tensor(f"in_{name}", a.shape, mybir.dt.from_np(a.dtype), kind="ExternalInput").ap()
    out = nc.dram_tensor("out", (1, T, D), mybir.dt.float32, kind="ExternalOutput").ap()
    with build(nc, args, out):
        pass
    r = run_bass_kernel_spmd(nc, [arrays], core_ids=[0])
    return r.results[0]["out"]
```

```python
import math
from contextlib import ExitStack

import numpy as np

import concourse.bass as bass
from concourse import mybir

T, D = 256, 1024
P = 128
C = T // P
DB = D // P
HEADS, HD = 16, 64
NOPE, ROPE = 64, 32
QK = NOPE + ROPE
QR, KVR = 768, 256
NE, DE = 16, 512
EB = DE // P
NG, EPG = 4, 4
SSM_W, SSM_G, SSM_P, SSM_N = 512, 32, 64, 16
ST = SSM_G * SSM_P // P
AH, KVH, IH, ID = 8, 2, 8, 32
TOPK = 64
PH, PK, PD, PT_ = 8, 128, 128, 16
SEL = PH * PT_
EPS = 1e-6
BIG = 3.0e38
NEG = -1.0e30
TWO_PI_A, TWO_PI_B = 6.28125, 0.0019350051879882812
TWO_PI_C = 2 * math.pi - TWO_PI_A - TWO_PI_B
ROUND = 12582912.0
PI = 3.1415925

K_ID, K_TRI, K_ONE = 0, 128, 256
K_CAUSAL = 384
K_CHUNK = K_CAUSAL + 384
K_COS64 = K_CHUNK + 384
K_SIN64 = K_COS64 + 64
K_COS32 = K_SIN64 + 64
K_SIN32 = K_COS32 + 32
K_INV = K_SIN32 + 32
K_IOTA = K_INV + 16
K_N = K_IOTA + 16


def shape_constants():
    k = np.zeros((P, K_N), np.float32)
    p = np.arange(P)
    k[:, K_ID:K_ID + P] = np.eye(P)
    k[:, K_TRI:K_TRI + P] = p[:, None] <= p[None, :]
    k[:, K_ONE:K_ONE + P] = 1
    for base, unit in ((K_CAUSAL, 1), (K_CHUNK, 64)):
        for c in range(C):
            at = base + P * c
            keys = np.arange(P * (c + 1))
            ok = (p[:, None] + P * c) // unit >= keys[None, :] // unit
            k[:, at:at + P * (c + 1)] = np.where(ok, np.float32(BIG), np.float32(NEG))
    for base_c, base_s, dim in ((K_COS64, K_SIN64, 64), (K_COS32, K_SIN32, 32)):
        inv = np.float32(10000.0) ** (-np.arange(0, dim, 2, dtype=np.float32) / np.float32(dim))
        for c in range(C):
            ang = (p + P * c).astype(np.float32)[:, None] * inv.astype(np.float32)[None, :]
            h = dim // 2
            k[:, base_c + h * c:base_c + h * (c + 1)] = np.cos(ang)
            k[:, base_s + h * c:base_s + h * (c + 1)] = np.sin(ang)
    k[:, K_INV:K_INV + 16] = np.float32(10000.0) ** (-np.arange(16, dtype=np.float32) / np.float32(16))
    k[:, K_IOTA:K_IOTA + 16] = np.arange(16)
    return k


def build(nc, A, out):
    fp32, fp32r, i32, u32 = mybir.dt.float32, mybir.dt.float32r, mybir.dt.int32, mybir.dt.uint32
    ALU = mybir.AluOpType
    ACT = mybir.ActivationFunctionType
    AX = mybir.AxisListType
    ctx = ExitStack()
    ctx.enter_context(nc.allow_non_contiguous_dma(reason="a few small parameters are laid out by their load"))
    sems, counts = {}, {}

    def S(name):
        if name not in sems:
            sems[name] = ctx.enter_context(nc.semaphore(name))
        return sems[name]

    def sb(name, shape, dt=fp32):
        return ctx.enter_context(nc.sbuf_tensor(name, shape, dt))

    RING, SLAB = 3, 4096
    ring = sb("ring", [P, RING * SLAB])
    STAGES, UW = 3, 1024
    WH, WL = (sb(n, [P, STAGES, UW], fp32r) for n in ("weights_high", "weights_low"))
    HTH, HTL = (sb(n, [P, DB, T], fp32r) for n in ("tokens_high", "tokens_low"))
    ATH, ATL = (sb(n, [P, EB, T], fp32r) for n in ("hidden_high", "hidden_low"))
    consts = sb("consts", [P, K_N])
    X = sb("X", [P, C, D])
    Hm = sb("H", [P, C * D])
    HTm = sb("HT", [P, DB * T])
    MOD = sb("MOD", [P, 6 * D])
    GAIN = sb("GAIN", [P, D])
    AR = sb("AR", [P, 13312])
    cT = sb("cT", [P, DB])
    cN = sb("cN", [DB, P])
    rope_cs = sb("rope_cs", [P, 2, C, 16])
    pos_i = sb("pos_i", [P, C], i32)
    rw = sb("rw", [P, DB, NE])
    rb = sb("rb", [P, NE])
    bf = sb("bf", [P, HEADS])
    st = sb("st", [P, 16])
    PS = ctx.enter_context(nc.psum_tensor("PS", [P, 8, 512], fp32))

    ident = consts[:, K_ID:K_ID + P]
    tri = consts[:, K_TRI:K_TRI + P]
    ones = consts[:, K_ONE:K_ONE + P]

    H = Hm[:, :].rearrange("p (c d) -> p c d", c=C)
    HT = HTm[:, :].rearrange("p (b t) -> p b t", t=T)

    def ar(at, *shape):
        return view(AR, at, *shape)

    def view(t, at, *shape):
        n = int(np.prod(shape))
        v = t[:, at:at + n]
        if len(shape) == 1:
            return v
        names = "abcd"[:len(shape)]
        return v.rearrange("p (" + " ".join(names) + ") -> p " + " ".join(names),
                           **{x: s for x, s in zip(names[1:], shape[1:])})

    slabs, pieces, stages, experts_at = [], [], {}, {}
    cut_units, units, n_units, n_used = {}, [], [0], [0]

    def stream(name, w, kb, cols, kind="N"):
        stages[name] = []
        for c0, n in cols:
            r = len(slabs)
            ps = [(o, min(512, n - o)) for o in range(0, n, 512)]
            for o, m in ps:
                stages[name].append((len(pieces), r, o, m, kind))
                pieces.append(name)
            slabs.append(dict(src=w[:, c0:c0 + n].rearrange("(b p) n -> p b n", p=P), kb=kb, n=n,
                              release=("gemm_done", len(pieces)), pieces=len(pieces)))

    def stream_cut(name, w, kb, cols, kind="N"):
        stream(name, w, kb, cols, kind)
        cut_units[name] = []
        for at, (g, r, off, n, kind) in enumerate(stages[name]):
            if n < P:
                continue
            stages[name][at] = (g, r, off, n, kind + "3")
            in_piece = n // P if kind == "T" else kb // 2
            for j in range(in_piece):
                last = j == in_piece - 1
                n_used[0] += not last
                cut_units[name].append(dict(n=n_units[0], g=g, r=r, j=j, kind=kind,
                                            used=("gemm_done", g + 1) if last else ("cut_used", n_used[0])))
                units.append(cut_units[name][-1])
                n_units[0] += 1
            slabs[r]["release"] = ("cut_low", n_units[0])

    def unit_views(u):
        s = slabs[u["r"]]
        w = slab_view(u["r"], s["kb"], s["n"])
        v = w[:, :, P * u["j"]:P * u["j"] + P] if u["kind"] == "T" else w[:, 2 * u["j"]:2 * u["j"] + 2, :]
        b, n = v.shape[1], v.shape[2]
        return v, [x[:, u["n"] % STAGES, 0:b * n].rearrange("p (b n) -> p b n", n=n) for x in (WH, WL)]

    def stream_experts(layer):
        experts_at[layer] = len(slabs)

    def stages_before(r):
        return slabs[r - 1]["pieces"]

    def cols(n, step=512, at=0):
        return [(at + o, min(step, n - o)) for o in range(0, n, step)]

    stream("mod0", A["w_mod"][0], DB, cols(6 * D), "M")
    stream_cut("a_qk", A["a_w_in"][0], DB, cols(2 * D), "T")
    stream_cut("a_v", A["a_w_in"][0], DB, cols(D, at=2 * D) + [(3 * D, HEADS)])
    stream_cut("a_o", A["a_w_o"][0], DB, cols(D))
    stream_experts(0)
    stream("kvmod", A["kv_w_mod"], DB, cols(2 * D), "M")
    stream("mod1", A["w_mod"][1], DB, cols(6 * D), "M")
    stream("kv_down", A["kv_w_down"], DB, [(0, KVR + ROPE)])
    stream("kv_up", A["kv_w_up"], KVR // P, [(0, 2 * D)])
    stream_cut("b_dq", A["b_w_dq"][0], DB, cols(QR))
    stream_cut("b_uq", A["b_w_uq"][0], QR // P, cols(HEADS * QK))
    stream_cut("b_o", A["b_w_o"][0], DB, cols(D))
    stream_experts(1)
    stream("c_u", A["w_in_2"][0], DB, [(0, 512)])
    stream("c_p", A["w_in_2"][0], DB, [(512, 512), (1024, 512), (1536, 40)])
    stream("c_g", A["w_in_2"][0], DB, cols(2 * D, at=1576))
    stream("glu", A["w_glu_2"][0], SSM_W // P, [(0, SSM_W)])
    stream("ssm_up", A["w_ssm_up_2"][0], SSM_W // P, [(0, D)])
    stream("attn_up", A["w_attn_up_2"][0], SSM_W // P, [(0, D)])
    stream_cut("c_o", A["w_out_2"][0], DB, cols(D))
    stream_cut("peer_q", A["peer_wq_2"][0], DB, cols(2 * D), "T")

    evac_by = {name: "v" for name in ("mod0", "mod1", "kvmod", "a_o", "b_o", "c_o")}
    evac_at, n_by = [], {"v": 0, "a": 0}
    for g, name in enumerate(pieces):
        e = evac_by.get(name, "a")
        n_by[e] += 1
        evac_at.append(("evac_" + e, n_by[e]))

    pair_of = [4 if name == "c_g" else 2 * (g % 2) for g, name in enumerate(pieces)]
    before = [max((h for h in range(g) if pair_of[h] == pair_of[g]), default=None) for g in range(len(pieces))]

    def slab_view(r, kb, n):
        return ring[:, (r % RING) * SLAB:(r % RING) * SLAB + kb * n].rearrange("p (b n) -> p b n", n=n)

    def slab_loaded(eng, r):
        eng.wait_ge(S(f"slab{r % RING}"), 16 * (r // RING + 1))

    UPE = 3 * EB

    def raw(u):
        return ring[:, u * UW:(u + 1) * UW]

    def link(eng, ins, name):
        counts[name] = counts.get(name, 0) + 1
        ins.then_inc(S(name), 1)
        eng.wait_ge(S(name), counts[name])

    ATT = {
        "A": dict(Q=ar(0, 8, T), K=ar(2048, 8, T), V=ar(4096, C, D), O=ar(6144, 8, T), SC=ar(8192, 2, 1024),
                  PT=ar(10240, 2, 1024), heads=16, scale=1.0, mask=K_CAUSAL),
        "B": dict(Q=ar(7168, 16, T), K=ar(3072, 16, T), V=ar(11264, C, D), O=HT, SC=ar(0, 2, 1024),
                  PT=view(Hm, 0, 2, 1024), heads=16, scale=float(QK) ** -0.5, mask=K_CHUNK),
        "C": dict(Q=ar(6224, 4, T), K=ar(7248, 2, T), V=ar(0, C, 1064), O=ar(8528, 4, T), SC=ar(9552, 2, 1024),
                  PT=view(HTm, 0, 2, 1024), heads=8, scale=0.125, mask=None),
    }
    F, Ft, Fn = ar(12288, C, HEADS), ar(12320, C, HEADS), ar(12352, C, HEADS)
    NCT = ar(12384, T)
    Y, SG, HID = ar(0, C, D), ar(4096, 4, T), ar(2048, 2, T)
    RSC, RSEL, COMB = ar(5120, C, NE), ar(5152, C, NE), ar(5184, C, NE)
    RT = ar(5216, 512)
    RIDX = AR[:, 5728:5744].bitcast(u32).rearrange("p (c k) -> p c k", c=C)
    KM = ar(11264, 2 * D)
    KTOK = ar(0, C, HEADS, QK)
    CKV, CKVT = ar(7168, C, KVR + ROPE), ar(7744, 2, T)
    CQ, CQT = ar(0, C, QR), view(Hm, 0, QR // P, T)
    QTOK = ar(0, C, HEADS, QK)
    PROJ, U, UT = ar(0, C, 1064), ar(2128, C, SSM_W), ar(3152, 4, T)
    Y5, Y5T = ar(4176, C, SSM_W), ar(5200, 4, T)
    GATES = view(MOD, 0, C, 2 * D)
    BN = [ar(6224, ST, 32), ar(6736, ST, 32)]
    CN = [ar(7248, 4, P), ar(7760, 4, P)]
    BT = [ar(8272, 4, P), ar(8784, 4, P)]
    CT = [ar(9296, 4, P), ar(9808, 4, P)]
    PHASE = [(ar(6224, 4, T), ar(7248, 4, T)), (ar(4176, 4, T), ar(5200, 4, T))]
    POW = [[ar(12752 + 32 * k + 16 * x, ST) for x in range(2)] for k in range(8)]
    T1, T2 = ar(10320, 4, T), ar(11344, 4, T)
    Zr, Zi = view(MOD, 4096, 4, T), view(MOD, 5120, 4, T)
    Sr, Si = view(Hm, 0, 4, T), view(Hm, 1024, 4, T)
    SP_ = [ar(12368 + 16 * i, ST) for i in range(24)]
    KD = ar(11600, C, 2, 2, HD)
    KI4 = ar(12112, C, 4, ID)
    QIT, KIT = ar(7760, 2, T), ar(8272, T)
    RELU = view(Hm, 0, IH, T)
    SCORE, SLEFT = ar(12368, T), ar(12624, T)
    T8, WI = ar(12880, 8), ar(12888, IH)
    MASKC = ar(11600, C, T)
    M1, M2 = ar(9552, C, D), view(Hm, 0, C, D)
    PQT, KT, PSC = ar(0, 16, T), ar(4096, 16, PK), ar(6144, C, 16, PK)
    W2, CAND, PTMP = ar(10240, 2, PK), ar(10496, PT_, PT_), ar(10752, 2, PT_, PT_)
    KN = view(MOD, 0, 16, PD)
    V2, I2F = view(MOD, 2048, 2, PT_), view(MOD, 2080, 2, PT_)
    I2 = MOD[:, 2112:2144].bitcast(u32).rearrange("p (b k) -> p b k", b=2)
    BV, BI = view(MOD, 2144, PT_), MOD[:, 2160:2176].bitcast(u32)
    POS = MOD[:, 2176:2208].bitcast(u32).rearrange("p (b k) -> p b k", b=2)
    POSF, EIX = view(MOD, 2208, 2, PT_), view(MOD, 2240, 2, PT_)
    TV = view(MOD, 2304, C * PH, PT_)
    EXPERT = MOD[:, 3840:4096].bitcast(u32).rearrange("p (c k) -> p c k", c=C)
    GATE, DOT = view(MOD, 4096, C, SEL), view(MOD, 4352, C, SEL)
    PSUMS = view(MOD, 4608, C * PH)
    PICK = [MOD[:, 4624 + 8 * i:4632 + 8 * i].bitcast(u32) for i in range(2)]

    LHS = {"a_qk": HT, "a_o": ATT["A"]["O"], "b_dq": HT, "b_uq": CQT, "b_o": HT, "c_o": HT, "peer_q": HT}
    lhs_no = {n: i for i, n in enumerate(LHS)}
    lhs_no["a_v"] = lhs_no["a_qk"]

    def row_place(half, j):
        n = 8 * half + j
        return ring[:, D * n:D * (n + 1)] if n < RING * SLAB // D else ar((n - RING * SLAB // D) * D, D)

    TPJ, tp_n = {}, [0]

    def tp_job(name, batches):
        TPJ[name] = (tp_n[0], batches)
        tp_n[0] += len(batches)

    def tp_end(name):
        return TPJ[name][0] + len(TPJ[name][1])

    def both_chunks(name, src, dst, nb, w=P):
        bs = []
        for c in range(C):
            for f in range(0, nb, 4):
                m = min(4, nb - f)
                bs.append(([src[:, c, w * (f + i):w * (f + i + 1)] for i in range(m)],
                           dst[0:w, f:f + m, P * c:P * c + P], 1.0, c))
        tp_job(name, bs)

    flat = "p c h d -> p c (h d)"
    both_chunks("h_a", H, HT, DB)
    tp_job("cum", [([Fn[:, c, :] for c in range(C)], NCT[0:HEADS, :].rearrange("p (a k) -> p a k", a=C), 1.0, 0)])
    both_chunks("h_ffn0", H, HT, DB)
    both_chunks("h_kv", H, HT, DB)
    both_chunks("ckv", CKV, CKVT, 2)
    both_chunks("kB", KTOK.rearrange(flat), ATT["B"]["K"], HEADS, QK)
    both_chunks("h_b", H, HT, DB)
    both_chunks("cq", CQ, CQT, QR // P)
    both_chunks("qB", QTOK.rearrange(flat), ATT["B"]["Q"], HEADS, QK)
    both_chunks("h_ffn1", H, HT, DB)
    both_chunks("h_n1", H, HT, DB)
    both_chunks("u", U, UT, 4)
    tp_job("ssm_w", [([BN[x][:, 4 * b:4 * b + 4, :].rearrange("p a d -> p (a d)") for b in range(4)],
                      BT[x], 1.0, 0) for x in range(2)] +
           [([CN[x][:, b, :] for b in range(4)], CT[x], 1.0 - 2 * x, 0)
            for x in range(2)])
    both_chunks("y5", Y5, Y5T, 4)
    both_chunks("y5g", Y5, Y5T, 4)
    both_chunks("qC", PROJ, ATT["C"]["Q"], 4)
    both_chunks("kC", KD.rearrange("p c a b d -> p c (a b d)"), ATT["C"]["K"], 2)
    both_chunks("qi", PROJ[:, :, 768:1024], QIT, 2)
    both_chunks("ki", KI4.rearrange(flat), KIT.rearrange("p (a t) -> p a t", a=1), 1)
    both_chunks("merged", M1, HT, DB)
    tp_job("peer_k", [([KN[:, 4 * b + i, :] for i in range(4)],
                       KT[:, 4 * b:4 * b + 4, :], 1.0, 0) for b in range(4)])
    both_chunks("h_n2", H, HT, DB)

    gain_list = [("a", A["a_norm_g"][0]), ("ffn0", A["ffn_norm_g"][0]), ("kv", A["kv_norm_g"]),
                 ("b", A["b_norm_g"][0]), ("latent", A["kv_latent_g"]), ("q", A["b_q_norm_g"][0]),
                 ("ffn1", A["ffn_norm_g"][1]), ("final", A["final_norm_g"]), ("n1", A["norm1_g_2"][0]),
                 ("dskip", A["d_skip_2"][0]), ("n2", A["norm2_g_2"][0]), ("nf", A["norm_f_g_2"])]
    gain_no = {n: i for i, (n, _) in enumerate(gain_list)}
    h_no = {n: i + 1 for i, n in enumerate(["a", "ffn0", "kv", "b", "ffn1", "n1", "n2"])}
    x_no = {n: i + 1 for i, n in enumerate(["a_o", "moe0", "b_o", "moe1", "c_o", "peer"])}

    block = ctx.enter_context(nc.Block())

    def rows(w):
        return w.rearrange("(c p) d -> p c d", p=P)

    @block.sync
    def _(sp):
        sp.dma_start(cN[:, :], A["c"][0].rearrange("(b p) -> b p", p=P)).then_inc(S("c_in"), 16)

        def load_experts(layer, pieces_before):
            gate, up, down = (A[n][layer] for n in ("exp_w_gate", "exp_w_up", "exp_w_down"))

            def load_unit(e, u):
                if u < 2 * EB:
                    m = u // 2
                    dst = raw(u).rearrange("p (b n) -> p b n", n=P)
                    src = (gate, up)[u % 2][e].rearrange("(b p) n -> p b n", p=P)[:, :, P * m:P * (m + 1)]
                else:
                    k = u - 2 * EB
                    dst, src = raw(u), down[e][P * k:P * (k + 1), :]
                sp.dma_start(dst, src).then_inc(S(f"unit{u}"), 16)

            sp.wait_ge(S("gemm_done"), pieces_before)
            for u in range(UPE):
                load_unit(0, u)
            with sp.Fori(1, NE) as e:
                for u in range(UPE):
                    sp.wait_ge(S(f"split{layer}"), e * UPE + (u + 1 - UPE))
                    load_unit(e, u)

        for r, s in enumerate(slabs):
            for layer, at in experts_at.items():
                if r == at:
                    load_experts(layer, stages_before(r))
                if at <= r < at + RING:
                    sp.wait_ge(S(f"split{layer}"), NE * UPE - UPE + (r % RING + 1) * (SLAB // UW))
            if r >= RING:
                sp.wait_ge(S(slabs[r - RING]["release"][0]), slabs[r - RING]["release"][1])
            sp.dma_start(slab_view(r, s["kb"], s["n"]), s["src"]).then_inc(S(f"slab{r % RING}"), 16)
        for c in range(C):
            sp.wait_ge(S("result"), c + 1)
            sp.dma_start(rows(out[0])[:, c, :], H[:, c, :]).then_inc(S("out_written"), 16)
        sp.wait_ge(S("out_written"), 16 * C)

    @block.gpsimd
    def _(pool):
        def bcast(dst, src, name):
            pool.dma_start(dst, src.partition_broadcast(P)).then_inc(S(name), 16)

        def load_gain(n):
            i = gain_no[n]
            if i:
                pool.wait_ge(S("gain_used"), i)
            src = gain_list[i][1]
            bcast(GAIN[:, 0:src.shape[0]], src, "gain_in")

        load_gain("a")
        bcast(bf[:, :], A["a_b_f"][0], "small_in")
        bcast(rb[:, :], A["router_bias"], "small_in")
        pool.dma_start(rw[:, :, :], A["router_w"].rearrange("(b p) n -> p b n", p=P)).then_inc(S("small_in"), 16)
        pool.dma_start(pos_i[:, :], A["positions"][0].rearrange("(c p) -> p c", p=P)).then_inc(S("small_in"), 16)
        load_gain("ffn0")
        load_gain("kv")
        pool.wait_ge(S("x_ready"), x_no["moe0"])
        bcast(KM, A["kv_b_mod"], "kvb_in")
        bcast(MOD[:, :], A["b_mod"][1], "modb1_in")
        load_gain("b")
        load_gain("latent")
        load_gain("q")
        load_gain("ffn1")
        load_gain("final")
        pool.wait_ge(S("x_ready"), x_no["b_o"])
        for x in range(2):
            pool.memset(BN[x], 0.0).then_inc(S("ssm_zero"), 1)
            pool.memset(CN[x], 0.0).then_inc(S("ssm_zero"), 1)
        pool.wait_ge(S("ssm_zero"), 4)
        for x, (b_, c_) in enumerate((("b_re_2", "c_re_2"), ("b_im_2", "c_im_2"))):
            for g in range(2):
                pool.dma_start(BN[x][64 * g:64 * g + 64, :, 16 * g:16 * g + 16],
                               A[b_][0].rearrange("(t g) p n -> g p t n", g=2)[g]).then_inc(S("ssm_in"), 16)
            csrc = A[c_][0].rearrange("(b i g) n p -> i g n b p", b=4, i=4)
            for i in range(4):
                for g in range(2):
                    q = 32 * i + 16 * g
                    pool.dma_start(CN[x][q:q + 16, :, 64 * g:64 * g + 64], csrc[i, g]).then_inc(S("ssm_in"), 16)
        for g in range(2):
            q = slice(64 * g, 64 * g + 64)
            pool.dma_start(SP_[0][q, :], A["a_re_2"][0].rearrange("(t g) p -> g p t", g=2)[g]).then_inc(S("ssm_in"), 16)
            pool.dma_start(SP_[1][q, :], A["a_im_2"][0].rearrange("(t g) p -> g p t", g=2)[g]).then_inc(S("ssm_in"), 16)
            pool.dma_start(SP_[2][q, :], A["log_dt_2"][0].rearrange("(t g) -> g t", g=2)[g].partition_broadcast(64)
                           ).then_inc(S("ssm_in"), 16)
        load_gain("n1")
        load_gain("dskip")
        pool.wait_ge(S("powers"), 1)
        for b in range(1, 4):
            if b >= 2:
                pool.wait_ge(S("states"), b - 1)
            er_, ei_ = PHASE[b % 2]
            link(pool, pool.memset(er_[:, :, 0:1], 1.0), "pool")
            link(pool, pool.memset(ei_[:, :, 0:1], 0.0), "pool")
            for k in range(8):
                n = 1 << k
                for t0, tn in ((0, 4),) if n < P else ((0, 2), (2, 2)):
                    ta, tb = (GAIN[:, 512 + 256 * x:512 + 256 * x + tn * n].rearrange("p (t a) -> p t a", t=tn)
                              for x in range(2))
                    q = slice(4 * b + t0, 4 * b + t0 + tn)
                    pr, pi_ = (POW[k][x][:, q].rearrange("p (t a) -> p t a", a=1).to_broadcast((P, tn, n))
                               for x in range(2))
                    er0, ei0 = er_[:, t0:t0 + tn, 0:n], ei_[:, t0:t0 + tn, 0:n]
                    for x0, x1, o, op in ((pr, pi_, er_, ALU.subtract), (pi_, pr, ei_, ALU.add)):
                        pool.tensor_tensor(ta, er0, x0, ALU.mult)
                        link(pool, pool.tensor_tensor(tb, ei0, x1, ALU.mult), "pool")
                        link(pool, pool.tensor_tensor(o[:, t0:t0 + tn, n:2 * n], ta, tb, op), "pool")
            pool.sem_inc(S("phases"), 1)
        load_gain("n2")
        pool.wait_ge(S("x_ready"), x_no["c_o"])
        for half, k_ in enumerate(("peer_k1_2", "peer_k2_2")):
            pool.dma_start(KN[:, half::2, :], A[k_][0].rearrange("h n d -> n h d")).then_inc(S("peerk_in"), 16)
        load_gain("nf")
        pool.wait_ge(S("gemm_done"), len(pieces))
        pool.wait_ge(S("peer_sc"), 4 * C)
        for ph, (tab, c) in enumerate(((("peer_u_2", 0)), ("peer_u_2", 1), ("peer_v_2", 0), ("peer_v_2", 1))):
            def ask(i, half):
                if ph < 2:
                    pool.wait_ge(S("experts"), i + (8 * c + 1))
                    pool.wait_ge(S(f"rows_used{half}"), i + (8 * ph + 1))
                else:
                    pool.wait_ge(S(f"x_acc{half}"), i * 8 + (64 * c + 1))
                at = i * 16 + 8 * half
                pool.tensor_copy(PICK[half], EXPERT[:, c, slice(at, at + 8) if isinstance(at, int) else bass.ds(at, 8)]
                                 ).then_inc(S(f"picked{half}"), 1)
                pool.wait_ge(S(f"picked{half}"), i + (8 * ph + 1))
                pool.sem_inc(S("sets_asked"), 1)
                for j in range(8):
                    pool.indirect_dma_start(
                        out=row_place(half, j), out_offset=None, in_=A[tab][0],
                        in_offset=bass.IndirectOffsetOnAxis(ap=PICK[half][:, j:j + 1], axis=0),
                    ).then_inc(S(f"rows_in{half}"), 16)

            if ph == 2:
                for half in range(2):
                    pool.wait_ge(S(f"rows_used{half}"), 2 * (SEL // 16) + 1)
                    ask(0, half)
            with pool.Fori(int(ph == 2), SEL // 16) as i:
                for half in range(2):
                    ask(i, half)

    @block.tensor
    def _(pe):
        def tp(name, *waits, per_chunk=None):
            for w, n in waits:
                pe.wait_ge(S(w), n)
            first, batches = TPJ[name]
            for b, (srcs, dst, _s, c) in enumerate(batches):
                n = first + b
                if per_chunk and (b == 0 or c != batches[b - 1][3]):
                    pe.wait_ge(S(per_chunk[0]), C * (per_chunk[1] - 1) + c + 1)
                if n >= 4:
                    pe.wait_ge(S("tp_out"), n - 3)
                for i, src in enumerate(srcs):
                    w = src.shape[-1]
                    last = nc.tensor.transpose(PS[0:w, 4 + n % 4, P * i:P * i + P], src, ident)
                last.then_inc(S("tp_done"), 1)

        products = ((0, 0), (0, 1), (1, 0))
        tokens, hidden, weights = (HTH, HTL), (ATH, ATL), (WH, WL)

        def gemm3(name, g, pair):
            mine = [u for u in cut_units[name] if u["g"] == g]
            for u in mine:
                ws, j = unit_views(u)[1], u["j"]
                pe.wait_ge(S("cut_low"), u["n"] + 1)
                if u["kind"] == "T":
                    pe.wait_ge(S("lhs_cut"), C * lhs_no[name] + C)
                    steps = [(k, a, b) for k in range(ws[0].shape[1]) for a, b in products]
                    o = T * (j % 2)
                    for i, (k, a, b) in enumerate(steps):
                        last = nc.tensor.matmul(PS[:, pair + j // 2, o:o + T], ws[a][:, k, :], tokens[b][:, k, :],
                                                start=i == 0, stop=i == len(steps) - 1)
                else:
                    n = ws[0].shape[2]
                    for c in range(C):
                        if j == 0:
                            pe.wait_ge(S("lhs_cut"), C * lhs_no[name] + c + 1)
                        for k in range(2):
                            for i, (a, b) in enumerate(products):
                                last = nc.tensor.matmul(
                                    PS[:, pair + c, 0:n], tokens[b][:, 2 * j + k, P * c:P * c + P], ws[a][:, k, :],
                                    start=j == 0 and k == 0 and i == 0, stop=u is mine[-1] and k == 1 and i == 2)
                last.then_inc(S(u["used"][0]), 1)

        def gemm(name, lhs, *waits, only=slice(None)):
            for w, n in waits:
                pe.wait_ge(S(w), n)
            for g, r, off, n, kind in stages[name][only]:
                s = slabs[r]
                if kind in ("N", "T", "M"):
                    slab_loaded(pe, r)
                if before[g] is not None:
                    pe.wait_ge(S(evac_at[before[g]][0]), evac_at[before[g]][1])
                w = slab_view(r, s["kb"], s["n"])
                pair = pair_of[g]
                if kind == "N":
                    for c in range(C):
                        for k in range(s["kb"]):
                            last = nc.tensor.matmul(PS[:, pair + c, 0:n], lhs[:, k, P * c:P * c + P],
                                                    w[:, k, off:off + n], start=k == 0, stop=k == s["kb"] - 1)
                elif kind == "T":
                    for f in range(n // P):
                        o = T * (f % 2)
                        for k in range(s["kb"]):
                            last = nc.tensor.matmul(PS[:, pair + f // 2, o:o + T], w[:, k, P * f:P * f + P],
                                                    lhs[:, k, :], start=k == 0, stop=k == s["kb"] - 1)
                elif kind[1:] == "3":
                    gemm3(name, g, pair)
                    continue
                else:
                    for k in range(s["kb"]):
                        last = nc.tensor.matmul(PS[:, pair, 0:n], cT[:, k:k + 1].to_broadcast((P, P)),
                                                w[:, k, off:off + n], start=k == 0, stop=k == s["kb"] - 1)
                last.then_inc(S("gemm_done"), 1)

        def ht(name):
            return ("tp_out", tp_end(name))

        def attention(a, first_waits):
            z = ATT[a]
            for w, n in first_waits:
                pe.wait_ge(S(w), n)
            steps = [(g, c) for g in range(z["heads"] // 4) for c in range(C)]

            def scores(n):
                g, c = steps[n]
                if n >= 2:
                    pe.wait_ge(S(f"masked{a}"), n - 1)
                kl = P * (c + 1)
                for i in range(4):
                    h = 4 * g + i
                    o = PS[:, 2 * (n % 2) + i % 2, T * (i // 2):T * (i // 2) + kl]
                    if a == "B":
                        q, k = z["Q"][0:QK, h, P * c:P * c + P], z["K"][0:QK, h, 0:kl]
                    else:
                        b = slice(64 * (h % 2), 64 * (h % 2) + 64)
                        kb = h // 2 if a == "A" else h // 4
                        q, k = z["Q"][b, h // 2, P * c:P * c + P], z["K"][b, kb, 0:kl]
                    last = nc.tensor.matmul(o, q, k, start=True, stop=a != "A")
                    if a == "A":
                        last = nc.tensor.matmul(o, ident[0:HEADS, h:h + 1].to_broadcast((HEADS, P)),
                                                NCT[0:HEADS, 0:kl], start=False, stop=True)
                last.then_inc(S(f"scores{a}"), 1)

            def transposes(n):
                g, c = steps[n]
                pe.wait_ge(S(f"probs{a}"), n + 1)
                if n >= 1:
                    pe.wait_ge(S(f"pt{a}"), n)
                sc = z["SC"][:, n % 2, 0:4 * P * (c + 1)].rearrange("p (h k) -> p h k", h=4)
                for i in range(4):
                    for kc in range(c + 1):
                        m = i * (c + 1) + kc
                        last = nc.tensor.transpose(PS[:, 4 + m // 4, P * (m % 4):P * (m % 4) + P],
                                                   sc[:, i, P * kc:P * kc + P], ident)
                last.then_inc(S(f"ptp{a}"), 1)

            def values(n):
                g, c = steps[n]
                pe.wait_ge(S(f"pt{a}"), n + 1)
                if n >= 2:
                    pe.wait_ge(S(f"o{a}"), n - 1)
                for i in range(4):
                    h = 4 * g + i
                    for kc in range(c + 1):
                        m = (2 * (i % 2) + i // 2) * (c + 1) + kc
                        at = 640 + (h // 4) * 64 if a == "C" else h * 64
                        last = nc.tensor.matmul(
                            PS[64 * (i % 2):64 * (i % 2) + 64, 6 + n % 2, P * (i // 2):P * (i // 2) + P],
                            z["V"][:, kc, at:at + 64], z["PT"][:, n % 2, P * m:P * m + P],
                            start=kc == 0, stop=kc == c)
                last.then_inc(S(f"omm{a}"), 1)

            scores(0)
            for n in range(len(steps)):
                if n + 1 < len(steps):
                    scores(n + 1)
                transposes(n)
                if n >= 1:
                    values(n - 1)
            values(len(steps) - 1)

        def experts(layer):
            pe.wait_ge(S("small_in"), 64)
            pe.wait_ge(S("tp_out"), tp_end(f"h_ffn{layer}"))
            for c in range(C):
                for k in range(DB):
                    last = nc.tensor.matmul(PS[:, 7, NE * c:NE * c + NE], HT[:, k, P * c:P * c + P], rw[:, k, :],
                                            start=k == 0, stop=k == DB - 1)
            last.then_inc(S("router_mm"), 1)
            pe.wait_ge(S("router_sig"), layer + 1)
            pe.wait_ge(S("ht_split"), layer + 1)
            with pe.Fori(0, NE) as e:
                for u in range(UPE):
                    pe.wait_ge(S(f"split{layer}"), e * UPE + (u + 1))
                    if u < 2 * EB:
                        m, x = u // 2, u % 2
                        if x == 0:
                            pe.wait_ge(S(f"act{layer}"), e * EB + (m + 1))
                        for k in range(DB):
                            for n, (a, b) in enumerate(products):
                                last = nc.tensor.matmul(PS[:, m, T * x:T * x + T],
                                                        weights[a][:, u % STAGES, P * k:P * k + P], tokens[b][:, k, :],
                                                        start=k == 0 and n == 0, stop=k == DB - 1 and n == 2)
                    else:
                        k = u - 2 * EB
                        pe.wait_ge(S(f"act{layer}"), e * EB + (k + 1 + EB))
                        for i in range(4):
                            c, half = i // 2, i % 2
                            if k == 0:
                                pe.wait_ge(S(f"y_done{layer}"), e * 4 + (i + 1))
                            for n, (a, b) in enumerate(products):
                                last = nc.tensor.matmul(
                                    PS[:, 4 + i, :], hidden[b][:, k, P * c:P * c + P],
                                    weights[a][:, u % STAGES, 512 * half:512 * half + 512],
                                    start=k == 0 and n == 0, stop=k == EB - 1 and n == 2)
                    last.then_inc(S(f"used{layer}"), 1)

        pe.wait_ge(S("consts_in"), 16)
        pe.wait_ge(S("c_silu"), 1)
        nc.tensor.transpose(PS[:, 7, 0:DB], cN[:, :], ident[0:DB, 0:DB]).then_inc(S("c_tp"), 1)
        gemm("mod0", None, ("c_act", 1))
        tp("h_a", per_chunk=("h_ready", h_no["a"]))
        gemm("a_qk", None)
        gemm("a_v", HT)
        pe.wait_ge(S("logf"), 1)
        for c in range(C):
            nc.tensor.matmul(PS[:, 0, HEADS * c:HEADS * c + HEADS], tri, F[:, c, :], start=True, stop=c == 0)
            if c:
                last = nc.tensor.matmul(PS[:, 0, HEADS * c:HEADS * c + HEADS], ones, F[:, 0, :],
                                        start=False, stop=True)
        last.then_inc(S("cum_mm"), 1)
        tp("cum", ("negcum", 1))
        attention("A", [ht("cum")])
        gemm("a_o", None)
        tp("h_ffn0", per_chunk=("h_ready", h_no["ffn0"]))
        experts(0)
        gemm("kvmod", None, ("x_ready", x_no["moe0"]))
        gemm("mod1", None)
        tp("h_kv", per_chunk=("h_ready", h_no["kv"]))
        gemm("kv_down", HT, ht("h_kv"))
        tp("ckv", per_chunk=("ckv", 1))
        gemm("kv_up", CKVT, ht("ckv"))
        tp("kB", ("krope", 1), evac_at[stages["kv_up"][-1][0]])
        tp("h_b", per_chunk=("h_ready", h_no["b"]))
        gemm("b_dq", None)
        tp("cq", per_chunk=("cq", 1))
        gemm("b_uq", None)
        tp("qB", per_chunk=("qrope", 1))
        attention("B", [ht("qB")])
        gemm("b_o", None)
        tp("h_ffn1", per_chunk=("h_ready", h_no["ffn1"]))
        experts(1)
        tp("h_n1", per_chunk=("h_ready", h_no["n1"]))
        gemm("c_u", HT, ht("h_n1"))
        gemm("c_p", HT)
        tp("u", evac_at[stages["c_u"][-1][0]])
        tp("ssm_w", ("ssm_b", 1))
        pe.wait_ge(S("tp_out"), tp_end("ssm_w"))

        def inputs(b):
            if b:
                pe.wait_ge(S("bu_read"), b)
            for x in range(2):
                for i in range(4):
                    q = slice(32 * i, 32 * i + 32)
                    last = nc.tensor.matmul(PS[:, i, T * x:T * x + T], BT[x][q, b, :],
                                            UT[q, b, :], start=True, stop=True, tile_position=(32 * i, 0))
            last.then_inc(S("bu"), 1)

        pe.wait_ge(S(evac_at[stages["c_p"][-1][0]][0]), evac_at[stages["c_p"][-1][0]][1])
        inputs(0)
        for b in range(4):
            gemm("c_g", HT, only=slice(b, b + 1))
            if b < 3:
                inputs(b + 1)
            pe.wait_ge(S("states"), b + 1)
            for i in range(4):
                for c in range(C):
                    o = PS[:, 6 + c, 32 * (4 * b + i):32 * (4 * b + i) + 32]
                    nc.tensor.matmul(o, Sr[:, i, P * c:P * c + P], CT[0][:, b, 32 * i:32 * i + 32],
                                     start=True, stop=False)
                    last = nc.tensor.matmul(o, Si[:, i, P * c:P * c + P], CT[1][:, b, 32 * i:32 * i + 32],
                                            start=False, stop=True)
            last.then_inc(S("y5_mm"), 1)
        pe.wait_ge(S(evac_at[stages["c_g"][-1][0]][0]), evac_at[stages["c_g"][-1][0]][1])
        tp("y5", ("y5", 1))
        gemm("glu", Y5T, ht("y5"))
        tp("y5g", ("y5g", 1))
        tp("qC", ("ropeC", 1))
        tp("kC")
        tp("qi")
        tp("ki")
        pe.wait_ge(S("tp_out"), tp_end("ki"))
        for c in range(C):
            if c:
                pe.wait_ge(S("index_read"), c)
            kl = P * (c + 1)
            for h in range(IH):
                q = slice(32 * (h % 4), 32 * (h % 4) + 32)
                last = nc.tensor.matmul(PS[:, h % 4, T * (h // 4):T * (h // 4) + kl],
                                        QIT[q, h // 4, P * c:P * c + P], KIT[q, 0:kl], start=True, stop=True,
                                        tile_position=(32 * (h % 4), 0))
            last.then_inc(S("index_mm"), 1)
        attention("C", [("index_read", 2)])
        gemm("ssm_up", Y5T, ("oC", 4))
        gemm("attn_up", ATT["C"]["O"])
        tp("merged", per_chunk=("merged", 1))
        gemm("c_o", None)
        tp("peer_k", ("peerk_in", 32))
        tp("h_n2", per_chunk=("h_ready", h_no["n2"]))
        gemm("peer_q", None)
        pe.wait_ge(S(evac_at[-1][0]), evac_at[-1][1])
        for c in range(C):
            for b in range(16):
                if b % 4 == 0 and c:
                    pe.wait_ge(S("peer_sc"), 4 * (c - 1) + b // 4 + 1)
                last = nc.tensor.matmul(PS[:, b // 4, P * (b % 4):P * (b % 4) + P], PQT[:, b, P * c:P * c + P],
                                        KT[:, b, :], start=True, stop=True)
                if b % 4 == 3:
                    last.then_inc(S("peer_mm"), 1)

    @block.scalar
    def _(act):
        A_ = nc.scalar.activation

        def tp(name):
            first, batches = TPJ[name]
            for b, (srcs, dst, scale, _) in enumerate(batches):
                n = first + b
                act.wait_ge(S("tp_done"), n + 1)
                w = srcs[0].shape[-1]
                A_(dst, PS[0:w, 4 + n % 4, 0:P * len(srcs)].rearrange("p (a k) -> p a k", k=P), ACT.Copy, scale=scale).then_inc(S("tp_out"), 1)

        def highs(name, first=0, end=None):
            for u in cut_units[name][first:end]:
                src, (high, _) = unit_views(u)
                slab_loaded(act, u["r"])
                if u["n"] >= STAGES:
                    act.wait_ge(S(units[u["n"] - STAGES]["used"][0]), units[u["n"] - STAGES]["used"][1])
                A_(high, src, ACT.Copy).then_inc(S("cut_high"), 1)

        def evac(name, fn, after=None):
            def out(i):
                g, r, off, n, kind = stages[name][i]
                act.wait_ge(S("gemm_done"), g + 1)
                fn(i, PS[:, pair_of[g]:pair_of[g] + 2, 0:n]).then_inc(S("evac_a"), 1)

            for i, (g, *_) in enumerate(stages[name]):
                mine = [k for k, u in enumerate(cut_units.get(name, ())) if u["g"] == g and k >= STAGES]
                if mine:
                    highs(name, mine[0], mine[-1] + 1)
                if i:
                    out(i - 1)
            if after:
                highs(after, 0, STAGES)
            out(len(stages[name]) - 1)

        def to_rows(dst, at=0):
            def fn(i, banks, dst=dst):
                n = banks.shape[-1]
                return A_(dst[:, :, at + 512 * i:at + 512 * i + n], banks, ACT.Copy)
            return fn

        def attention(a):
            z = ATT[a]
            steps = [(g, c) for g in range(z["heads"] // 4) for c in range(C)]

            def exps(n):
                g, c = steps[n]
                act.wait_ge(S(f"negmax{a}"), n + 1)
                sc = z["SC"][:, n % 2, 0:4 * P * (c + 1)].rearrange("p (h k) -> p h k", h=4)
                for i in range(4):
                    last = A_(sc[:, i, :], sc[:, i, :], ACT.Exp, bias=st[:, 4 * (n % 2) + i:4 * (n % 2) + i + 1],
                              accum_out=st[:, 8 + 4 * (n % 2) + i:8 + 4 * (n % 2) + i + 1])
                last.then_inc(S(f"exp{a}"), 1)

            def pt(n):
                c = steps[n][1]
                act.wait_ge(S(f"ptp{a}"), n + 1)
                if n >= 2:
                    act.wait_ge(S(f"omm{a}"), n - 1)
                m = 512 * (c + 1)
                A_(z["PT"][:, n % 2, 0:m].rearrange("p (b k) -> p b k", k=512), PS[:, 4:4 + c + 1, :],
                   ACT.Copy).then_inc(S(f"pt{a}"), 1)

            def o(n):
                g, c = steps[n]
                act.wait_ge(S(f"omm{a}"), n + 1)
                A_(z["O"][:, 2 * g:2 * g + 2, P * c:P * c + P],
                   PS[:, 6 + n % 2, 0:2 * P].rearrange("p (a k) -> p a k", a=2), ACT.Copy).then_inc(S(f"o{a}"), 1)

            N = len(steps)
            for n in range(N + 2):
                if n < N:
                    exps(n)
                if 1 <= n <= N:
                    pt(n - 1)
                if n >= 2:
                    o(n - 2)

        def high(layer, e, u):
            act.wait_ge(S(f"unit{u}"), e * 16 + 16 * (NE * layer + 1))
            act.wait_ge(S(f"used{layer}"), e * UPE + (u + 1))
            A_(WH[:, u % STAGES, :], raw(u), ACT.Copy).then_inc(S(f"high{layer}"), 1)

        def experts(layer):
            act.wait_ge(S("router_mm"), layer + 1)
            A_(RSC.rearrange("p c e -> p (c e)"), PS[:, 7, 0:C * NE], ACT.Sigmoid).then_inc(S("router_sig"), 1)

            def expert(e, more):
                for u in range(UPE):
                    if u + 2 < UPE:
                        high(layer, e, u + 2)
                    elif more:
                        high(layer, e + 1, u + 2 - UPE)
                    if u < 2 * EB and u % 2:
                        m = u // 2
                        act.wait_ge(S(f"used{layer}"), e * UPE + (u + 1 + STAGES))
                        act.wait_ge(S(f"act{layer}"), e * EB + (m + 1))
                        A_(SG[:, m, :], PS[:, m, 0:T], ACT.Silu).then_inc(S(f"silu{layer}"), 1)

            with act.Fori(0, NE - 1) as e:
                expert(e, True)
            expert(NE - 1, False)

        act.dma_start(consts[:, :], A["consts"]).then_inc(S("consts_in"), 16)
        act.dma_start(MOD[:, :], A["b_mod"][0].partition_broadcast(P)).then_inc(S("modb_in"), 16)
        act.dma_start(X[:, :, :], rows(A["x"][0])).then_inc(S("x_in"), 16)
        act.wait_ge(S("c_in"), 16)
        A_(cN[:, :], cN[:, :], ACT.Silu).then_inc(S("c_silu"), 1)
        act.wait_ge(S("c_tp"), 1)
        A_(cT[:, :], PS[:, 7, 0:DB], ACT.Copy).then_inc(S("c_act"), 1)
        highs("a_qk", 0, STAGES)
        tp("h_a")
        z = ATT["A"]

        def qk_out(i, banks):
            dst = (z["Q"] if i < 2 else z["K"])[:, 4 * (i % 2):4 * (i % 2) + 4, :]
            return A_(dst.rearrange("p (u a) t -> p u (a t)", u=2), banks, ACT.Copy, scale=0.125 if i < 2 else 1.0)
        evac("a_qk", qk_out, after="a_v")
        evac("a_v", lambda i, banks: to_rows(z["V"])(i, banks) if i < 2 else A_(F, banks, ACT.Copy))
        act.wait_ge(S("ang"), 1)
        A_(rope_cs[:, 1, :, :], rope_cs[:, 0, :, :], ACT.Sin).then_inc(S("sin"), 1)
        act.wait_ge(S("sin"), 1)
        A_(rope_cs[:, 0, :, :], rope_cs[:, 0, :, :], ACT.Sin, scale=0.5).then_inc(S("sin"), 1)
        act.wait_ge(S("f_abs"), 1)
        A_(Ft, Ft, ACT.Exp, scale=-1.0).then_inc(S("f_exp"), 1)
        act.wait_ge(S("f_exp"), 1)
        A_(Ft, Ft, ACT.Ln, bias=ones[:, 0:1]).then_inc(S("f_ln"), 1)
        act.wait_ge(S("cum_mm"), 1)
        A_(Fn, PS[:, 0, 0:C * HEADS].rearrange("p (c h) -> p c h", c=C), ACT.Copy, scale=-1.0).then_inc(S("negcum"), 1)
        tp("cum")
        highs("a_o", 0, STAGES)
        attention("A")
        highs("a_o", STAGES)
        for u in range(2):
            high(0, 0, u)
        tp("h_ffn0")
        experts(0)
        tp("h_kv")
        evac("kv_down", lambda i, banks: A_(CKV, banks, ACT.Copy))
        tp("ckv")

        def kv_out(i, banks):
            b = banks.rearrange("p c (h d) -> p c h d", h=4)
            for c in range(C):
                A_(KTOK[:, c, 4 * i:4 * i + 4, 0:NOPE], b[:, c, :, 0:NOPE], ACT.Copy)
            return A_(ATT["B"]["V"][:, :, 256 * i:256 * i + 256].rearrange("p c (h d) -> p c h d", h=4),
                      b[:, :, :, NOPE:P], ACT.Copy)
        evac("kv_up", kv_out)
        tp("kB")
        act.wait_ge(S("used0"), STAGES + NE * UPE)
        highs("b_dq", 0, STAGES)
        tp("h_b")
        evac("b_dq", to_rows(CQ), after="b_uq")
        tp("cq")
        evac("b_uq", to_rows(QTOK.rearrange(flat)))
        tp("qB")
        highs("b_o", 0, STAGES)
        attention("B")
        highs("b_o", STAGES)
        for u in range(2):
            high(1, 0, u)
        tp("h_ffn1")
        experts(1)
        act.wait_ge(S("ssm_in"), 16 * (2 * 2 + 8 * 2 + 6))
        A_(SP_[2], SP_[2], ACT.Exp).then_inc(S("dt"), 1)
        tp("h_n1")
        evac("c_u", to_rows(U))
        act.wait_ge(S("ssm_ang"), 1)
        A_(SP_[6], SP_[3], ACT.Exp)
        A_(SP_[7], SP_[5], ACT.Sin)
        A_(SP_[8], SP_[5], ACT.Sin, scale=0.5).then_inc(S("ssm_sin"), 1)
        evac("c_p", to_rows(PROJ))
        tp("u")
        tp("ssm_w")
        evac("c_g", lambda i, banks: A_(GATES[:, :, 512 * i:512 * i + 512], banks, ACT.Sigmoid))
        act.wait_ge(S("y5_pre"), 1)
        A_(Y5, Y5, ACT.Gelu_apprx_tanh).then_inc(S("y5"), 1)
        tp("y5")
        evac("glu", lambda i, banks: A_(U, banks, ACT.Sigmoid))
        tp("y5g")
        tp("qC")
        tp("kC")
        tp("qi")
        tp("ki")
        attention("C")
        evac("ssm_up", to_rows(M1))
        act.wait_ge(S("used1"), STAGES + NE * UPE)
        highs("c_o", 0, STAGES)
        evac("attn_up", to_rows(M2))
        tp("merged")
        highs("c_o", STAGES)
        highs("peer_q", 0, STAGES)
        tp("peer_k")
        tp("h_n2")
        evac("peer_q", lambda i, banks: A_(PQT[:, 4 * i:4 * i + 4, :].rearrange("p (u a) t -> p u (a t)", u=2), banks,
                                           ACT.Copy))
        for c in range(C):
            for q in range(4):
                act.wait_ge(S("peer_mm"), 4 * c + q + 1)
                A_(PSC[:, c, 4 * q:4 * q + 4, :].rearrange("p a k -> p (a k)"), PS[:, q, :], ACT.Copy
                   ).then_inc(S("peer_sc"), 1)
        act.wait_ge(S("top_shift"), 1)
        A_(TV, TV, ACT.Exp).then_inc(S("top_exp"), 1)
        for half in range(2):
            act.wait_ge(S(f"rows_used{half}"), 2 * (SEL // 16) + 1)
        A_(DOT, DOT, ACT.Gelu_apprx_tanh).then_inc(S("gelu"), 1)

    @block.vector
    def _(dve):
        V = nc.vector

        def L(ins):
            link(dve, ins, "v")

        def tt(o, a, b, op):
            L(V.tensor_tensor(o, a, b, op))

        def ts(o, a, s1, op0, s2=None, op1=None):
            if op1 is None:
                L(V.tensor_scalar(o, a, s1, None, op0))
            else:
                L(V.tensor_scalar(o, a, s1, s2, op0, op1))

        def wait(name, n):
            dve.wait_ge(S(name), n)

        def inverse_root(y, v, t):
            L(V.tensor_single_scalar(t.bitcast(i32), v.bitcast(i32), 1, ALU.logical_shift_right))
            ts(y.bitcast(i32), t.bitcast(i32), -1.0, ALU.mult, float(0x5F3759DF), ALU.add)
            for _ in range(3):
                tt(t, y, v, ALU.mult)
                L(V.scalar_tensor_tensor(t, t, -0.5, y, ALU.mult, ALU.mult))
                L(V.scalar_tensor_tensor(y, t, 1.5, y, ALU.add, ALU.mult))

        def scale_gain(gname, scale):
            wait("gain_in", 16 * (gain_no[gname] + 1))
            L(V.scalar_tensor_tensor(GAIN[:, :], scale, 1.0, GAIN[:, :], ALU.add, ALU.mult))

        def rms(src, width, dst, gname, junk=None, shift=None, signal=None, again=False):
            wait("gain_in", 16 * (gain_no[gname] + 1))
            junk = dst if junk is None else junk
            if not again:
                V.scalar_tensor_tensor(junk[:, 0, 0:width], src[:, 0, :], 1.0, src[:, 0, :], ALU.mult, ALU.mult,
                                       accum_out=st[:, 0:1])
                L(V.scalar_tensor_tensor(junk[:, 1, 0:width], src[:, 1, :], 1.0, src[:, 1, :], ALU.mult, ALU.mult,
                                         accum_out=st[:, 1:2]))
                ts(st[:, 2:4], st[:, 0:2], 1.0 / width, ALU.mult, EPS, ALU.add)
                inverse_root(st[:, 4:6], st[:, 2:4], st[:, 6:8])
            for c in range(C):
                last = V.scalar_tensor_tensor(dst[:, c, :], src[:, c, :], st[:, 4 + c:5 + c],
                                              GAIN[:, 0:width], ALU.mult, ALU.mult)
                if shift is not None:
                    L(last)
                    last = V.tensor_tensor(dst[:, c, :], dst[:, c, :], shift, ALU.add)
                if signal:
                    last.then_inc(S(signal), 1)
                    counts[signal] = counts.get(signal, 0) + 1
                else:
                    L(last)
            if signal:
                wait(signal, counts[signal])
            dve.sem_inc(S("gain_used"), 1)

        def mod_part(i):
            return MOD[:, D * i:D * (i + 1)]

        def add_bias(name, dst, first=0, end=None):
            for i, (g, r, off, n, kind) in list(enumerate(stages[name]))[first:end]:
                wait("gemm_done", g + 1)
                V.tensor_tensor(dst[:, 512 * i:512 * i + n], PS[:, 2 * (g % 2), 0:n], dst[:, 512 * i:512 * i + n],
                                ALU.add).then_inc(S("evac_v"), 1)
            wait("evac_v", evac_at[g][1])

        def wait_evac(name):
            e = evac_at[stages[name][-1][0]]
            wait(*e)

        def gated_add(y, gate, ready):
            for c in range(C):
                L(V.tensor_tensor(y[:, c, :], y[:, c, :], gate, ALU.mult))
            V.tensor_tensor(X[:, :, :], X[:, :, :], y, ALU.add).then_inc(S("x_ready"), 1)
            wait("x_ready", x_no[ready])

        def add_product(name, gate):
            for i, (g, r, off, n, kind) in enumerate(stages[name]):
                wait("gemm_done", g + 1)
                banks, x = PS[:, 2 * (g % 2):2 * (g % 2) + 2, :], X[:, :, 512 * i:512 * i + 512]
                if gate is not None:
                    t = H[:, :, 512 * i:512 * i + 512]
                    V.tensor_tensor(t, banks, gate[:, 512 * i:512 * i + 512].rearrange("p (a d) -> p a d", a=1)
                                    .to_broadcast((P, C, 512)), ALU.mult).then_inc(S("evac_v"), 1)
                    wait("evac_v", evac_at[g][1])
                    last = V.tensor_tensor(x, x, t, ALU.add)
                    if i == 0:
                        L(last)
                else:
                    last = V.tensor_tensor(x, x, banks, ALU.add).then_inc(S("evac_v"), 1)
                    wait("evac_v", evac_at[g][1])
            if gate is not None:
                last.then_inc(S("x_ready"), 1)
                wait("x_ready", x_no[name])
            else:
                dve.sem_inc(S("x_ready"), 1)

        def reduce_angle(a, t):
            ts(t, a, 1.0 / (2 * math.pi), ALU.mult)
            ts(t, t, ROUND, ALU.add)
            ts(t, t, ROUND, ALU.subtract)
            for k in (TWO_PI_A, TWO_PI_B, TWO_PI_C):
                L(V.scalar_tensor_tensor(a, t, -k, a, ALU.mult, ALU.add))
            ts(a, a, PI, ALU.min, -PI, ALU.max)

        def rope(x1, x2, cos, sin, t, signal="v"):
            tt(t[0], x1, cos, ALU.mult)
            tt(t[1], x2, sin, ALU.mult)
            tt(t[2], x2, cos, ALU.mult)
            tt(t[3], x1, sin, ALU.mult)
            tt(x1, t[0], t[1], ALU.subtract)
            link(dve, V.tensor_tensor(x2, t[2], t[3], ALU.add), signal)

        def attention(a, out=None):
            z = ATT[a]
            steps = [(g, c) for g in range(z["heads"] // 4) for c in range(C)]

            def mask(n):
                g, c = steps[n]
                kl = P * (c + 1)
                wait(f"scores{a}", n + 1)
                if n >= 2:
                    wait(f"ptp{a}", n - 1)
                sc = z["SC"][:, n % 2, 0:4 * kl].rearrange("p (h k) -> p h k", h=4)
                ps = PS[:, 2 * (n % 2):2 * (n % 2) + 2, :].rearrange("p b (x k) -> p (b x) k", x=2)[:, :, 0:kl]
                if z["mask"] is None:
                    m, op = MASKC[:, c, 0:kl], ALU.add
                else:
                    m, op = consts[:, z["mask"] + P * c:z["mask"] + P * c + kl], ALU.min
                V.scalar_tensor_tensor(sc, ps, z["scale"],
                                       m.rearrange("p (a k) -> p a k", a=1).to_broadcast((P, 4, kl)), ALU.mult, op
                                       ).then_inc(S(f"masked{a}"), 1)
                wait(f"masked{a}", n + 1)
                V.tensor_reduce(st[:, 4 * (n % 2):4 * (n % 2) + 4], sc, AX.X, ALU.max, negate=True
                                ).then_inc(S(f"negmax{a}"), 1)

            def norm(n):
                g, c = steps[n]
                kl = P * (c + 1)
                wait(f"exp{a}", n + 1)
                r = st[:, 8 + 4 * (n % 2):12 + 4 * (n % 2)]
                L(V.reciprocal(r, r))
                sc = z["SC"][:, n % 2, 0:4 * kl].rearrange("p (h k) -> p h k", h=4)
                V.tensor_tensor(sc, sc, r.rearrange("p (h a) -> p h a", a=1).to_broadcast((P, 4, kl)), ALU.mult
                                ).then_inc(S(f"probs{a}"), 1)

            mask(0)
            for n in range(len(steps)):
                if n + 1 < len(steps):
                    mask(n + 1)
                norm(n)
                if out and n < STAGES:
                    lows(out, n, n + 1)
            wait(f"probs{a}", len(steps))

        def lows(name, first=0, end=None):
            for u in cut_units[name][first:end]:
                src, (high, low) = unit_views(u)
                wait("cut_high", u["n"] + 1)
                V.tensor_tensor(low, src, high.bitcast(fp32), ALU.subtract).then_inc(S("cut_low"), 1)

        def cut_lhs(name, ready, *n):
            kb = LHS[name].shape[1]
            for c in range(C):
                wait(ready, n[c])
                value, high, low = (x[:, 0:kb, P * c:P * c + P] for x in (LHS[name], HTH, HTL))
                L(V.tensor_copy(high, value))
                V.tensor_tensor(low, value, high.bitcast(fp32), ALU.subtract).then_inc(S("lhs_cut"), 1)

        def chunks_out(name):
            first, batches = TPJ[name]
            return [first + len(batches) * (c + 1) // C for c in range(C)]

        def experts(layer):
            def low(e, u):
                wait(f"high{layer}", e * UPE + (u + 1))
                V.tensor_tensor(WL[:, u % STAGES, :], raw(u), WH[:, u % STAGES, :].bitcast(fp32), ALU.subtract
                                ).then_inc(S(f"split{layer}"), 1)

            for u in range(2):
                low(0, u)
            wait("tp_out", tp_end(f"h_ffn{layer}"))
            L(V.tensor_copy(HTH[:, :, :], HT))
            V.tensor_tensor(HTL[:, :, :], HT, HTH[:, :, :].bitcast(fp32), ALU.subtract).then_inc(S("ht_split"), 1)
            wait("router_sig", layer + 1)
            tt(RSEL, RSC, rb[:, :].rearrange("p (a e) -> p a e", a=1).to_broadcast((P, C, NE)), ALU.add)
            q = RSEL.rearrange("p c (g e) -> p c g e", e=EPG)
            def tmp(i, n=C * NG):
                return RT[:, 32 * i:32 * i + n]
            def g4(i):
                return tmp(i).rearrange("p (c g) -> p c g", c=C)
            tt(g4(0), q[:, :, :, 0], q[:, :, :, 1], ALU.max)
            tt(g4(1), q[:, :, :, 0], q[:, :, :, 1], ALU.min)
            tt(g4(2), q[:, :, :, 2], q[:, :, :, 3], ALU.max)
            tt(g4(3), q[:, :, :, 2], q[:, :, :, 3], ALU.min)
            tt(g4(4), g4(0), g4(2), ALU.max)
            tt(g4(5), g4(0), g4(2), ALU.min)
            tt(g4(1), g4(1), g4(3), ALU.max)
            tt(g4(5), g4(5), g4(1), ALU.max)
            tt(g4(4), g4(4), g4(5), ALU.add)
            best = RT[:, 192:194]
            L(V.tensor_reduce(best, g4(4), AX.X, ALU.max))
            tt(g4(0), g4(4), best.rearrange("p (c a) -> p c a", a=1).to_broadcast((P, C, NG)), ALU.is_equal)
            for c in range(C):
                L(V.tensor_tensor_scan(g4(1)[:, c, :], ones[:, 0:NG], g4(0)[:, c, :], 0.0, ALU.mult, ALU.add))
            L(V.scalar_tensor_tensor(g4(0), g4(1), 1.0, g4(0), ALU.is_equal, ALU.mult))
            ts(g4(1), g4(0), 1.0, ALU.subtract, -NEG, ALU.mult)
            for c in range(C):
                qc = RSEL[:, c, :].rearrange("p (g e) -> p g e", e=EPG)
                tt(qc, qc, g4(1)[:, c, :].rearrange("p (g a) -> p g a", a=1).to_broadcast((P, NG, EPG)), ALU.add)
            top8 = RT[:, 200:216].rearrange("p (c k) -> p c k", c=C)
            idx = RT[:, 216:232].rearrange("p (c k) -> p c k", c=C)
            for c in range(C):
                L(V.max(top8[:, c, :], RSEL[:, c, :]))
                L(V.max_index(RIDX[:, c, :], top8[:, c, :], RSEL[:, c, :]))
            L(V.tensor_copy(idx, RIDX))
            oh = [RT[:, 256 + 32 * i:288 + 32 * i].rearrange("p (c e) -> p c e", c=C) for i in range(2)]
            iota = consts[:, K_IOTA:K_IOTA + NE].rearrange("p (a e) -> p a e", a=1).to_broadcast((P, C, NE))
            for i in range(2):
                tt(oh[i], iota, idx[:, :, i:i + 1].to_broadcast((P, C, NE)), ALU.is_equal)
            tt(oh[0], oh[0], oh[1], ALU.add)
            tt(COMB, oh[0], RSC, ALU.mult)
            L(V.tensor_reduce(best, COMB, AX.X, ALU.add))
            L(V.reciprocal(best, best))
            tt(COMB, COMB, best.rearrange("p (c a) -> p c a", a=1).to_broadcast((P, C, NE)), ALU.mult)
            L(V.memset(Y, 0.0))
            dve.sem_inc(S(f"y_done{layer}"), 4)

            def expert(e, more):
                for u in range(UPE):
                    if u + 2 < UPE:
                        low(e, u + 2)
                    elif more:
                        low(e + 1, u + 2 - UPE)
                    if u < 2 * EB and u % 2:
                        m = u // 2
                        wait(f"silu{layer}", e * EB + (m + 1))
                        hid, high = HID[:, m % 2, :], ATH[:, m, :]
                        V.tensor_tensor(hid, SG[:, m, :], PS[:, m, T:2 * T], ALU.mult).then_inc(S(f"hid{layer}"), 1)
                        wait(f"hid{layer}", e * 2 * EB + (2 * m + 1))
                        V.tensor_copy(high, hid).then_inc(S(f"hid{layer}"), 1)
                        wait(f"hid{layer}", e * 2 * EB + (2 * m + 2))
                        V.tensor_tensor(ATL[:, m, :], hid, high.bitcast(fp32), ALU.subtract
                                        ).then_inc(S(f"act{layer}"), 1)
                wait(f"used{layer}", e * UPE + (UPE + STAGES))
                for i in range(4):
                    c, half = i // 2, i % 2
                    y = Y[:, c, 512 * half:512 * half + 512]
                    wait(f"y_done{layer}", e * 4 + (i + 1))
                    w = COMB[:, c, e:e + 1] if isinstance(e, int) else COMB[:, c, bass.ds(e, 1)]
                    V.scalar_tensor_tensor(y, PS[:, 4 + i, :], w, y, ALU.mult, ALU.add
                                           ).then_inc(S(f"y_done{layer}"), 1)

            with dve.Fori(0, NE - 1) as e:
                expert(e, True)
            expert(NE - 1, False)
            wait(f"y_done{layer}", 4 * NE + 4)

        for layer in range(2):
            dve.sem_inc(S(f"act{layer}"), EB)
            dve.sem_inc(S(f"used{layer}"), STAGES)
        L(V.memset(st[:, :], 0.0))
        wait("modb_in", 16)
        add_bias("mod0", MOD, 0, 4)
        wait("x_in", 16)
        scale_gain("a", mod_part(1))
        rms(X, D, H, "a", shift=mod_part(0), signal="h_ready")
        add_bias("mod0", MOD, 4)
        lows("a_qk", 0, STAGES)
        cut_lhs("a_qk", "tp_out", *chunks_out("h_a"))
        lows("a_qk", STAGES)
        wait("small_in", 64)
        posf = st[:, 14:16]
        L(V.tensor_copy(posf, pos_i[:, :]))
        RA, RB_ = rope_cs[:, 0, :, :], rope_cs[:, 1, :, :]
        tt(RA, posf.rearrange("p (c a) -> p c a", a=1).to_broadcast((P, C, 16)),
           consts[:, K_INV:K_INV + 16].rearrange("p (a k) -> p a k", a=1).to_broadcast((P, C, 16)), ALU.mult)
        reduce_angle(RA, RB_)
        dve.sem_inc(S("ang"), 1)
        lows("a_v")
        wait_evac("a_v")
        tt(F, F, bf[:, :].rearrange("p (a h) -> p a h", a=1).to_broadcast((P, C, HEADS)), ALU.add)
        V.scalar_tensor_tensor(Ft, F, -1.0, F, ALU.mult, ALU.max).then_inc(S("f_abs"), 1)
        ts(F, F, 0.0, ALU.min)
        wait("f_ln", 1)
        V.tensor_tensor(F, F, Ft, ALU.subtract).then_inc(S("logf"), 1)
        attention("A", out="a_o")
        cut_lhs("a_o", "oA", 7, 8)
        lows("a_o", STAGES)
        scale_gain("ffn0", mod_part(4))
        add_product("a_o", mod_part(2))
        rms(X, D, H, "ffn0", shift=mod_part(3), signal="h_ready")
        experts(0)
        gated_add(Y, mod_part(5), "moe0")
        wait("sin", 2)
        tt(RA, RA, RA, ALU.mult)
        ts(RA, RA, -2.0, ALU.mult, 1.0, ALU.add)
        wait("kvb_in", 16)
        add_bias("kvmod", KM)
        scale_gain("kv", KM[:, D:2 * D])
        rms(X, D, H, "kv", shift=KM[:, 0:D], signal="h_ready")
        wait("modb1_in", 16)
        add_bias("mod1", MOD)
        scale_gain("b", mod_part(1))
        wait("tp_out", tp_end("h_kv"))
        rms(X, D, H, "b", shift=mod_part(0), signal="h_ready", again=True)
        wait_evac("kv_down")
        heads = "p (a h) -> p a h"
        for c in range(C):
            rt = [view(HTm, 16 * i, 16) for i in range(4)]
            rope(CKV[:, c, KVR:KVR + 16], CKV[:, c, KVR + 16:KVR + 32], rope_cs[:, 0, c, :], rope_cs[:, 1, c, :], rt)
        for c in range(C):
            last = V.tensor_copy(KTOK[:, c, :, NOPE:QK],
                                 CKV[:, c, KVR:KVR + 32].rearrange("p (a r) -> p a r", a=1).to_broadcast((P, HEADS, ROPE)))
            if c == 0:
                L(last)
        last.then_inc(S("krope"), 1)
        rms(CKV[:, :, 0:KVR], KVR, CKV[:, :, 0:KVR], "latent", junk=HTm[:, 0:512].rearrange("p (c d) -> p c d", c=C),
            signal="ckv")
        lows("b_dq", 0, STAGES)
        cut_lhs("b_dq", "tp_out", *chunks_out("h_b"))
        lows("b_dq", STAGES)
        lows("b_uq", 0, STAGES)
        wait_evac("b_dq")
        rms(CQ, QR, CQ, "q", junk=HTm[:, 0:2 * QR].rearrange("p (c d) -> p c d", c=C), signal="cq")
        cut_lhs("b_uq", "tp_out", *chunks_out("cq"))
        lows("b_uq", STAGES)
        wait_evac("b_uq")
        for c in range(C):
            rt = [view(HTm, 256 * i, HEADS, 16) for i in range(4)]
            cs = [rope_cs[:, k, c, :].rearrange("p (a r) -> p a r", a=1).to_broadcast((P, HEADS, 16)) for k in range(2)]
            rope(QTOK[:, c, :, NOPE:NOPE + 16], QTOK[:, c, :, NOPE + 16:QK], cs[0], cs[1], rt, signal="qrope")
        wait("tp_out", tp_end("qB"))
        attention("B", out="b_o")
        cut_lhs("b_o", "oB", 7, 8)
        lows("b_o", STAGES)
        scale_gain("ffn1", mod_part(4))
        add_product("b_o", mod_part(2))
        rms(X, D, H, "ffn1", shift=mod_part(3), signal="h_ready")
        experts(1)
        gated_add(Y, mod_part(5), "moe1")
        rms(X, D, X, "final", junk=H)
        rms(X, D, H, "n1", signal="h_ready")
        lr, li, dt, x, t, ang, ex, sn, sh, xc, p_, m_, em, cm, r_, ar_, ai_, dd, fr, fi, er, u_ = SP_[:22]
        wait("dt", 1)
        tt(x, lr, dt, ALU.mult)
        tt(ang, li, dt, ALU.mult)
        reduce_angle(ang, t)
        V.tensor_copy(st[:, 9:10], st[:, 8:9]).then_inc(S("ssm_ang"), 1)
        ts(xc, x, 0.5, ALU.min, -0.5, ALU.max)
        ts(p_, xc, 1.0 / 8, ALU.mult, 1.0, ALU.add)
        for k in (7, 6, 5, 4, 3, 2):
            tt(p_, p_, xc, ALU.mult)
            ts(p_, p_, 1.0 / k, ALU.mult, 1.0, ALU.add)
        tt(p_, p_, xc, ALU.mult)
        L(V.scalar_tensor_tensor(m_, x, -1.0, x, ALU.mult, ALU.max))
        ts(m_, m_, 0.5, ALU.is_lt)
        wait("ssm_sin", 1)
        ts(ex, ex, BIG, ALU.min, -1.0, ALU.add)
        tt(em, p_, ex, ALU.subtract)
        tt(em, em, m_, ALU.mult)
        tt(em, em, ex, ALU.add)
        tt(cm, sh, sh, ALU.mult)
        ts(cm, cm, -2.0, ALU.mult)
        ts(r_, em, 1.0, ALU.add)
        tt(ar_, r_, cm, ALU.mult)
        tt(ar_, ar_, em, ALU.add)
        tt(ai_, r_, sn, ALU.mult)
        tt(dd, lr, lr, ALU.mult)
        tt(t, li, li, ALU.mult)
        tt(dd, dd, t, ALU.add)
        L(V.reciprocal(dd, dd))
        for o, a1, b1, a2, b2, op in ((fr, ar_, lr, ai_, li, ALU.add), (fi, ai_, lr, ar_, li, ALU.subtract)):
            tt(o, a1, b1, ALU.mult)
            tt(t, a2, b2, ALU.mult)
            tt(o, o, t, op)
            tt(o, o, dd, ALU.mult)
        ts(er, cm, 1.0, ALU.add)
        frb, fib = (f.rearrange("p (t a) -> p t a", a=1).to_broadcast((P, ST, 32)) for f in (fr, fi))
        w4 = [ar(10320 + 512 * i, ST, 32) for i in range(4)]
        tt(w4[0], BN[0], frb, ALU.mult)
        tt(w4[1], BN[1], fib, ALU.mult)
        tt(w4[2], BN[1], frb, ALU.mult)
        tt(w4[3], BN[0], fib, ALU.mult)
        tt(BN[0], w4[0], w4[1], ALU.subtract)
        V.tensor_tensor(BN[1], w4[2], w4[3], ALU.add).then_inc(S("ssm_b"), 1)
        L(V.tensor_copy(POW[0][0], er))
        L(V.tensor_copy(POW[0][1], sn))
        for k in range(7):
            (a_, b_), (a2_, b2_) = POW[k], POW[k + 1]
            tt(a2_, a_, a_, ALU.mult)
            tt(t, b_, b_, ALU.mult)
            tt(a2_, a2_, t, ALU.subtract)
            tt(t, a_, b_, ALU.mult)
            ts(b2_, t, 2.0, ALU.mult)
        dve.sem_inc(S("powers"), 1)
        wait_evac("c_p")
        for c in range(C):
            for at, n, h, kc_, ks_ in ((0, 10, 32, K_COS64, K_SIN64), (768, 9, 16, K_COS32, K_SIN32)):
                v = PROJ[:, c, at:at + 2 * h * n].rearrange("p (n d) -> p n d", n=n)
                cs = [consts[:, k + h * c:k + h * c + h].rearrange("p (a r) -> p a r", a=1).to_broadcast((P, n, h))
                      for k in (kc_, ks_)]
                rope(v[:, :, 0:h], v[:, :, h:2 * h], cs[0], cs[1], [ar(10320 + 512 * i, n, h) for i in range(4)])
        def first_phases(Er, Ei):
            L(V.memset(Er[:, :, 0:1], 1.0))
            L(V.memset(Ei[:, :, 0:1], 0.0))
            for k in range(8):
                n = 1 << k
                pr, pi_ = (POW[k][x_][:, 0:4].rearrange("p (t a) -> p t a", a=1).to_broadcast((P, 4, n)) for x_ in range(2))
                V.tensor_tensor(T1[:, :, 0:n], Er[:, :, 0:n], pr, ALU.mult)
                V.tensor_tensor(T2[:, :, 0:n], Ei[:, :, 0:n], pi_, ALU.mult)
                V.tensor_tensor(Zr[:, :, 0:n], Er[:, :, 0:n], pi_, ALU.mult)
                tt(Zi[:, :, 0:n], Ei[:, :, 0:n], pr, ALU.mult)
                V.tensor_tensor(Er[:, :, n:2 * n], T1[:, :, 0:n], T2[:, :, 0:n], ALU.subtract)
                tt(Ei[:, :, n:2 * n], Zr[:, :, 0:n], Zi[:, :, 0:n], ALU.add)

        wait("tp_out", tp_end("ssm_w"))
        wait("tp_out", tp_end("h_n1"))
        for b in range(4):
            q = slice(4 * b, 4 * b + 4)
            Er, Ei = PHASE[b % 2]
            if b:
                wait("phases", b)
            else:
                first_phases(Er, Ei)
            wait("bu", b + 1)
            br, bi = (PS[:, 0:4, T * x_:T * x_ + T] for x_ in range(2))
            V.tensor_tensor(T1, br, Er, ALU.mult)
            V.tensor_tensor(T2, bi, Ei, ALU.mult)
            V.tensor_tensor(Zr, bi, Er, ALU.mult)
            V.tensor_tensor(Zi, br, Ei, ALU.mult).then_inc(S("bu_read"), 1)
            wait("bu_read", b + 1)
            tt(T1, T1, T2, ALU.add)
            tt(T2, Zr, Zi, ALU.subtract)
            for i in range(4):
                rr = r_[:, 4 * b + i:4 * b + i + 1].to_broadcast((P, T))
                V.tensor_tensor_scan(Zr[:, i, :], rr, T1[:, i, :], 0.0, ALU.mult, ALU.add)
                last = V.tensor_tensor_scan(Zi[:, i, :], rr, T2[:, i, :], 0.0, ALU.mult, ALU.add)
            L(last)
            V.tensor_tensor(T1, Zr, Er, ALU.mult)
            tt(T2, Zi, Ei, ALU.mult)
            if b:
                wait("y5_mm", b)
            tt(Sr, T1, T2, ALU.subtract)
            V.tensor_tensor(T1, Zr, Ei, ALU.mult)
            tt(T2, Zi, Er, ALU.mult)
            V.tensor_tensor(Si, T1, T2, ALU.add).then_inc(S("states"), 1)
            wait("states", b + 1)
        wait("gain_in", 16 * (gain_no["dskip"] + 1))
        V.tensor_tensor(Y5, U, GAIN[:, 0:SSM_W].rearrange("p (a d) -> p a d", a=1).to_broadcast((P, C, SSM_W)), ALU.mult
                        ).then_inc(S("gain_used"), 1)
        wait("gain_used", gain_no["dskip"] + 1)
        wait("y5_mm", 4)
        V.tensor_tensor(Y5, Y5, PS[:, 6:8, :], ALU.add).then_inc(S("y5_pre"), 1)
        wait_evac("glu")
        V.tensor_tensor(Y5, Y5, U, ALU.mult).then_inc(S("y5g"), 1)
        for c in range(C):
            L(V.tensor_copy(KD[:, c, :, :, :], PROJ[:, c, 512:640].rearrange("p (k a d) -> p k a d", k=2, a=1)
                            .to_broadcast((P, 2, 2, HD))))
            last = V.tensor_copy(KI4[:, c, :, :], PROJ[:, c, 1024:1056].rearrange("p (a d) -> p a d", a=1)
                                 .to_broadcast((P, 4, ID)))
            if c == 0:
                L(last)
        last.then_inc(S("ropeC"), 1)
        wait("tp_out", tp_end("ki"))
        for c in range(C):
            kl = P * (c + 1)
            wait("index_mm", c + 1)
            ps = PS[:, 0:4, :].rearrange("p b (x k) -> p (b x) k", x=2)[:, :, 0:kl]
            L(V.tensor_copy(WI.rearrange("p (b x) -> p b x", x=2), PROJ[:, c, 1056:1064].rearrange("p (x b) -> p b x", x=2)))
            V.scalar_tensor_tensor(RELU[:, :, 0:kl], ps, 0.0,
                                   WI.rearrange("p (h a) -> p h a", a=1).to_broadcast((P, IH, kl)),
                                   ALU.max, ALU.mult).then_inc(S("index_read"), 1)
            wait("index_read", c + 1)
            sc, left = SCORE[:, 0:kl], SLEFT[:, 0:kl]
            clamp = consts[:, K_CAUSAL + P * c:K_CAUSAL + P * c + kl]
            L(V.tensor_reduce(sc, RELU[:, :, 0:kl].rearrange("p h k -> p k h"), AX.X, ALU.add))
            L(V.scalar_tensor_tensor(sc, sc, (IH * ID) ** -0.5, clamp, ALU.mult, ALU.min))
            for k in range(TOPK // 8):
                L(V.max(T8, left if k else sc))
                L(V.match_replace(left, T8, left if k else sc, -BIG))
            tt(MASKC[:, c, 0:kl], left, sc, ALU.is_equal)
            L(V.scalar_tensor_tensor(MASKC[:, c, 0:kl], MASKC[:, c, 0:kl], NEG, clamp, ALU.mult, ALU.min))
        attention("C")
        lows("c_o", 0, STAGES)
        wait_evac("attn_up")
        V.tensor_tensor(M1, M1, GATES[:, :, 0:D], ALU.mult)
        tt(M2, M2, GATES[:, :, D:2 * D], ALU.mult)
        for c in range(C):
            V.tensor_tensor(M1[:, c, :], M1[:, c, :], M2[:, c, :], ALU.add).then_inc(S("merged"), 1)
        cut_lhs("c_o", "tp_out", *chunks_out("merged"))
        lows("c_o", STAGES)
        add_product("c_o", None)
        rms(X, D, H, "n2", signal="h_ready")
        lows("peer_q", 0, STAGES)
        cut_lhs("peer_q", "tp_out", *chunks_out("h_n2"))
        lows("peer_q", STAGES)
        for half in range(2):
            dve.sem_inc(S(f"rows_used{half}"), 1)
            dve.sem_inc(S(f"x_acc{half}"), 1)
        iota = consts[:, K_IOTA:K_IOTA + PT_].rearrange("p (b a e) -> p b a e", a=1, b=1
                                                        ).to_broadcast((P, 2, PT_, PT_))
        LINKS = 17

        def cols_of(h, width):
            return slice(h * width, (h + 1) * width) if isinstance(h, int) else bass.ds(h * width, width)

        def select(c, h):
            n = [0]

            def M(ins):
                n[0] += 1
                ins.then_inc(S("select"), 1)
                wait("select", h * LINKS + (8 * c * LINKS + n[0]))

            def best16(*tables):
                for k in range(2):
                    for op in ("values", "places", "remove")[0:3 - k]:
                        dve.sem_inc(S("select_seen"), 1)
                        for values, indices, table in tables:
                            v8, i8 = values[:, 8 * k:8 * k + 8], indices[:, 8 * k:8 * k + 8]
                            if op == "values":
                                last = V.max(v8, table)
                            elif op == "places":
                                last = V.max_index(i8, v8, table)
                            else:
                                last = V.match_replace(table, v8, table, -BIG)
                        M(last)

            def over(x, axis):
                return x.rearrange("p (i a) -> p i a" if axis else "p (a i) -> p a i", a=1).to_broadcast((P, PT_, PT_))

            def over2(x, axis):
                return x.rearrange("p b (i a) -> p b i a" if axis else "p b (a i) -> p b a i", a=1
                                   ).to_broadcast((P, 2, PT_, PT_))

            M(V.tensor_copy(W2.rearrange("p a k -> p (a k)"),
                            PSC[:, c, :, :].rearrange("p b k -> p (b k)")[:, cols_of(h, 2 * PK)]))
            best16(*((V2[:, half, :], I2[:, half, :], W2[:, half, :]) for half in range(2)))
            V.tensor_copy(I2F, I2)
            M(V.tensor_tensor(CAND, over(V2[:, 0, :], 1), over(V2[:, 1, :], 0), ALU.add))
            best16((BV, BI, CAND.rearrange("p i j -> p (i j)")))
            V.tensor_copy(TV[:, 8 * c:8 * c + 8, :].rearrange("p h k -> p (h k)")[:, cols_of(h, PT_)], BV)
            V.tensor_single_scalar(POS[:, 0, :], BI, 4, ALU.logical_shift_right)
            M(V.tensor_single_scalar(POS[:, 1, :], BI, 15, ALU.bitwise_and))
            M(V.tensor_copy(POSF, POS))
            M(V.tensor_tensor(PTMP, iota, over2(POSF, 1), ALU.is_equal))
            M(V.tensor_tensor(PTMP, PTMP, over2(I2F, 0), ALU.mult))
            M(V.tensor_reduce(EIX, PTMP, AX.X, ALU.add))
            assert n[0] == LINKS, n
            V.scalar_tensor_tensor(EXPERT[:, c, cols_of(h, PT_)], EIX[:, 0, :], float(PK), EIX[:, 1, :],
                                   ALU.mult, ALU.add).then_inc(S("experts"), 1)

        def dots(c, h):
            for half in range(2):
                wait(f"rows_in{half}", h * P + P * (8 * c + 1))
                for j in range(8):
                    at = h * PT_ + (8 * half + j)
                    last = V.scalar_tensor_tensor(row_place(half, j), row_place(half, j), 1.0, H[:, c, :], ALU.mult, ALU.mult,
                                                  accum_out=DOT[:, c, slice(at, at + 1) if isinstance(at, int)
                                                                else bass.ds(at, 1)])
                last.then_inc(S(f"rows_used{half}"), 1)

        for c in range(C):
            wait("peer_sc", 4 * (c + 1))
            select(c, 0)
            if c:
                dots(0, PH - 1)
            with dve.Fori(1, PH) as h:
                select(c, h)
                dots(c, h - 1)
        wait("experts", C * PH)
        L(V.tensor_copy(PSUMS, TV[:, :, 0]))
        V.tensor_tensor(TV, TV, PSUMS.rearrange("p (h a) -> p h a", a=1).to_broadcast((P, C * PH, PT_)), ALU.subtract
                        ).then_inc(S("top_shift"), 1)
        dots(1, PH - 1)
        wait("top_exp", 1)
        L(V.tensor_reduce(PSUMS, TV, AX.X, ALU.add))
        L(V.reciprocal(PSUMS, PSUMS))
        tt(GATE.rearrange("p c (h k) -> p (c h) k", h=PH), TV,
           PSUMS.rearrange("p (h a) -> p h a", a=1).to_broadcast((P, C * PH, PT_)), ALU.mult)
        wait("gelu", 1)
        tt(DOT, DOT, GATE, ALU.mult)
        for c in range(C):
            with dve.Fori(0, SEL // 16) as i:
                for half in range(2):
                    wait(f"rows_in{half}", i * P + P * (16 + 8 * c + 1))
                    for j in range(8):
                        n = 8 * half + j
                        V.scalar_tensor_tensor(X[:, c, :], row_place(half, j), DOT[:, c, bass.ds(i * 16 + n, 1)], X[:, c, :],
                                               ALU.mult, ALU.add).then_inc(S(f"x_acc{half}"), 1)
                        wait(f"x_acc{half}", i * 8 + (64 * c + j + 2))
            wait("gain_in", 16 * (gain_no["nf"] + 1))
            L(V.scalar_tensor_tensor(H[:, c, :], X[:, c, :], 1.0, X[:, c, :], ALU.mult, ALU.mult,
                                     accum_out=st[:, 0:1]))
            ts(st[:, 2:3], st[:, 0:1], 1.0 / D, ALU.mult, EPS, ALU.add)
            inverse_root(st[:, 4:5], st[:, 2:3], st[:, 6:7])
            V.scalar_tensor_tensor(H[:, c, :], X[:, c, :], st[:, 4:5], GAIN[:, :], ALU.mult, ALU.mult
                                   ).then_inc(S("result"), 1)
            wait("result", c + 1)

    return ctx


INPUTS = ["x", "c", "positions", "a_norm_g", "a_w_in", "a_b_f", "a_w_o", "kv_norm_g", "kv_w_mod", "kv_b_mod",
          "kv_w_down", "kv_latent_g", "kv_w_up", "b_norm_g", "b_w_dq", "b_q_norm_g", "b_w_uq", "b_w_o", "w_mod",
          "b_mod", "ffn_norm_g", "router_w", "router_bias", "exp_w_gate", "exp_w_up", "exp_w_down", "final_norm_g",
          "norm1_g_2", "w_in_2", "a_re_2", "a_im_2", "log_dt_2", "b_re_2", "b_im_2", "c_re_2", "c_im_2", "d_skip_2",
          "w_glu_2", "w_ssm_up_2", "w_attn_up_2", "w_out_2", "norm2_g_2", "peer_wq_2", "peer_k1_2", "peer_k2_2",
          "peer_u_2", "peer_v_2", "norm_f_g_2"]


def kernel(**inputs):
    import concourse.bacc as bacc
    from concourse.bass_utils import run_bass_kernel_spmd

    nc = bacc.Bacc("TRN2", target_bir_lowering=False, num_devices=1)
    arrays, args = {}, {}
    given = {name: np.ascontiguousarray(inputs[name]) for name in INPUTS}
    given["consts"] = shape_constants()
    for name, a in given.items():
        arrays[f"in_{name}"] = a
        args[name] = nc.dram_tensor(f"in_{name}", a.shape, mybir.dt.from_np(a.dtype), kind="ExternalInput").ap()
    out = nc.dram_tensor("out", (1, T, D), mybir.dt.float32, kind="ExternalOutput").ap()
    with build(nc, args, out):
        pass
    r = run_bass_kernel_spmd(nc, [arrays], core_ids=[0])
    return r.results[0]["out"]
```
